# Optimizing a Trainium2 kernel written in Bass

```python
import jax, jax.numpy as jnp
from jax import lax
import numpy as np

D_MODEL = 1024
BATCH = 1
SEQ = 512
DEPTH = 2

CTX_LEN = 256
GRID_W = 64
N_POOL_GROUPS = 4
POOL_GROUP = 128
POOL_WIDTH = N_POOL_GROUPS * POOL_GROUP
POOL_WINDOWS = (2, 4, 8, 16)
GLA_HEADS = 4
GLA_DK = 64
GLA_DV = 128
GLA_KW = GLA_HEADS * GLA_DK
GLA_VW = GLA_HEADS * GLA_DV
GATE_RANK = 16
GATE_TAU = 16.0
CHUNK = 64
D_FF = 2816
N_MOD = 9
EPS = 1e-6

OFF_K = 0
OFF_V = OFF_K + GLA_KW
OFF_AF = OFF_V + GLA_VW
OFF_AB = OFF_AF + GATE_RANK
OFF_Q = OFF_AB + GATE_RANK
OFF_R = OFF_Q + GLA_KW
OFF_POOL = OFF_R + GLA_VW
OFF_GP = OFF_POOL + POOL_WIDTH
OFF_GG = OFF_GP + D_MODEL
IN_COLS = OFF_GG + D_MODEL

kernel_name = "hybrid_pool_gla_macaron_dit"

def rmsnorm(x, w):
    xf = x.astype(jnp.float32)
    y = xf * lax.rsqrt(jnp.mean(xf * xf, axis=-1, keepdims=True) + EPS)
    return (y * w.astype(jnp.float32)).astype(x.dtype)

def modulate(x, w, shift, scale):
    return rmsnorm(x, w) * (1 + scale) + shift

def modulation(cond, w_mod, b_mod):
    m = jax.nn.silu(cond) @ w_mod + b_mod
    return jnp.split(m, N_MOD, axis=-1)

def swiglu(h, w_up, w_down):
    a, b = jnp.split(h @ w_up, 2, axis=-1)
    return (jax.nn.silu(a) * b) @ w_down

def box_mean(u, w, axis):
    n = u.shape[axis]
    cs = jnp.cumsum(u.astype(jnp.float32), axis=axis)
    pad = [(0, 0)] * u.ndim
    pad[axis] = (1, 0)
    cs = jnp.pad(cs, pad)
    t = jnp.arange(n)
    lo = jnp.clip(t - w // 2, 0, n)
    hi = jnp.clip(t + w // 2, 0, n)
    s = jnp.take(cs, hi, axis=axis) - jnp.take(cs, lo, axis=axis)
    shape = [1] * u.ndim
    shape[axis] = n
    cnt = (hi - lo).astype(jnp.float32).reshape(shape)
    return (s / cnt).astype(u.dtype)

def pool_mix(u, grid, pool_w, pool_scale):
    B, L, _ = u.shape
    outs = []
    for gi, w in enumerate(POOL_WINDOWS):
        ug = u[..., gi * POOL_GROUP:(gi + 1) * POOL_GROUP]
        if grid:
            rows = L // GRID_W
            ugr = ug.reshape(B, rows, GRID_W, POOL_GROUP)
            m = box_mean(box_mean(ugr, w, 1), w, 2).reshape(B, L, POOL_GROUP)
        else:
            m = box_mean(ug, w, 1)
        outs.append(m - ug)
    p = jnp.stack(outs, axis=2)
    y = jnp.einsum('blgp,gpq->blgq', p, pool_w).reshape(B, L, POOL_WIDTH)
    return y * pool_scale

def to_heads(t, d):
    B, L, _ = t.shape
    return t.reshape(B, L, GLA_HEADS, d).transpose(0, 2, 1, 3)

def log_forget(a_low, w_up, b):
    return jax.nn.log_sigmoid((a_low @ w_up + b).astype(jnp.float32)) / GATE_TAU

def gla_kvg(proj, lp):
    k = to_heads(proj[..., OFF_K:OFF_V], GLA_DK)
    v = to_heads(proj[..., OFF_V:OFF_AF], GLA_DV)
    g_f = to_heads(log_forget(proj[..., OFF_AF:OFF_AB], lp['w_af_up'], lp['b_af']), GLA_DK)
    g_b = to_heads(log_forget(proj[..., OFF_AB:OFF_Q], lp['w_ab_up'], lp['b_ab']), GLA_DK)
    return k, v, g_f, g_b

def flip_seq(t):
    return jnp.flip(t, axis=2)

def gla_chunked(q, k, v, g, s0, inclusive):
    f32 = jnp.float32
    B, H, L, dk = q.shape
    dv = v.shape[-1]
    n = L // CHUNK
    qc = q.astype(f32).reshape(B, H, n, CHUNK, dk)
    kc = k.astype(f32).reshape(B, H, n, CHUNK, dk)
    vc = v.astype(f32).reshape(B, H, n, CHUNK, dv)
    b = jnp.cumsum(g.astype(f32).reshape(B, H, n, CHUNK, dk), axis=3)
    b_last = b[:, :, :, -1:, :]
    q_t = qc * jnp.exp(b)
    k_t = kc * jnp.exp(-b)
    k_end = kc * jnp.exp(b_last - b)
    mask = jnp.tril(jnp.ones((CHUNK, CHUNK), bool), 0 if inclusive else -1)
    att = jnp.where(mask, jnp.einsum('bhncd,bhnmd->bhncm', q_t, k_t), 0.0)
    o = jnp.einsum('bhncm,bhnme->bhnce', att, vc)
    kv = jnp.einsum('bhncd,bhnce->bhnde', k_end, vc)
    decay = jnp.exp(b_last[:, :, :, 0, :])

    def step(s, inp):
        kv_n, dec_n = inp
        return s * dec_n[..., None] + kv_n, s

    _, s_prev = lax.scan(step, s0.astype(f32), (jnp.moveaxis(kv, 2, 0), jnp.moveaxis(decay, 2, 0)))
    s_prev = jnp.moveaxis(s_prev, 0, 2)
    o = o + jnp.einsum('bhncd,bhnde->bhnce', q_t, s_prev)
    return o.reshape(B, H, L, dv).astype(v.dtype)

def gla_final_state(k, v, g):
    f32 = jnp.float32
    b = jnp.cumsum(g.astype(f32), axis=2)
    dec = jnp.exp(b[:, :, -1:, :] - b)
    return jnp.einsum('bhld,bhle->bhde', k.astype(f32) * dec, v.astype(f32))

def context_states(proj, lp):
    k, v, g_f, g_b = gla_kvg(proj, lp)
    s_f = gla_final_state(k, v, g_f)
    s_b = gla_final_state(flip_seq(k), flip_seq(v), flip_seq(g_b))
    return s_f, s_b

def gla_branch(proj, s_f0, s_b0, lp):
    k, v, g_f, g_b = gla_kvg(proj, lp)
    q = to_heads(proj[..., OFF_Q:OFF_R], GLA_DK) * (GLA_DK ** -0.5)
    o_f = gla_chunked(q, k, v, g_f, s_f0, True)
    o_b = flip_seq(gla_chunked(flip_seq(q), flip_seq(k), flip_seq(v), flip_seq(g_b), s_b0, False))
    o = rmsnorm(o_f + o_b, lp['gla_norm_w'])
    B, H, L, _ = o.shape
    o = o.transpose(0, 2, 1, 3).reshape(B, L, GLA_VW)
    return o * jax.nn.silu(proj[..., OFF_R:OFF_POOL])

def token_mixer(h, grid, s_f0, s_b0, lp):
    proj = h @ lp['w_in']
    y_gla = gla_branch(proj, s_f0, s_b0, lp) @ lp['w_br_gla']
    y_pool = pool_mix(proj[..., OFF_POOL:OFF_GP], grid, lp['pool_w'], lp['pool_scale']) @ lp['w_br_pool']
    merged = jax.nn.sigmoid(proj[..., OFF_GP:OFF_GG]) * y_pool + jax.nn.sigmoid(proj[..., OFF_GG:IN_COLS]) * y_gla
    return merged @ lp['w_out'], proj

def setup_inputs(seed: int = 0) -> dict:
    key = jax.random.key(seed)
    ks = jax.random.split(key, 24)
    f32 = jnp.float32
    L = DEPTH

    def nrm(k, shape, fan):
        return jax.random.normal(k, shape, f32) * (fan ** -0.5)

    def near_one(k, shape):
        return 1.0 + 0.02 * jax.random.normal(k, shape, f32)

    def small(k, shape, s):
        return s * jax.random.normal(k, shape, f32)

    return {
        "x": jax.random.normal(ks[0], (BATCH, SEQ, D_MODEL), f32),
        "c": jax.random.normal(ks[1], (BATCH, D_MODEL), f32),
        "ctx": jax.random.normal(ks[2], (BATCH, CTX_LEN, D_MODEL), f32),
        "c_ctx": jax.random.normal(ks[3], (D_MODEL,), f32),
        "w_mod": nrm(ks[4], (L, D_MODEL, N_MOD * D_MODEL), D_MODEL),
        "b_mod": small(ks[5], (L, N_MOD * D_MODEL), 0.02),
        "norm_w": near_one(ks[6], (L, 3, D_MODEL)),
        "ffn1_up": nrm(ks[7], (L, D_MODEL, 2 * D_FF), D_MODEL),
        "ffn1_down": nrm(ks[8], (L, D_FF, D_MODEL), D_FF),
        "w_in": nrm(ks[9], (L, D_MODEL, IN_COLS), D_MODEL),
        "w_af_up": nrm(ks[10], (L, GATE_RANK, GLA_KW), GATE_RANK),
        "b_af": small(ks[11], (L, GLA_KW), 0.1),
        "w_ab_up": nrm(ks[12], (L, GATE_RANK, GLA_KW), GATE_RANK),
        "b_ab": small(ks[13], (L, GLA_KW), 0.1),
        "gla_norm_w": near_one(ks[14], (L, GLA_DV)),
        "pool_w": nrm(ks[15], (L, N_POOL_GROUPS, POOL_GROUP, POOL_GROUP), POOL_GROUP),
        "pool_scale": near_one(ks[16], (L, POOL_WIDTH)),
        "w_br_pool": nrm(ks[17], (L, POOL_WIDTH, D_MODEL), POOL_WIDTH),
        "w_br_gla": nrm(ks[18], (L, GLA_VW, D_MODEL), GLA_VW),
        "w_out": nrm(ks[19], (L, D_MODEL, D_MODEL), D_MODEL),
        "ffn2_up": nrm(ks[20], (L, D_MODEL, 2 * D_FF), D_MODEL),
        "ffn2_down": nrm(ks[21], (L, D_FF, D_MODEL), D_FF),
        "final_norm_w": near_one(ks[22], (D_MODEL,)),
    }

def reference(x, c, ctx, c_ctx, w_mod, b_mod, norm_w, ffn1_up, ffn1_down, w_in, w_af_up, b_af,
              w_ab_up, b_ab, gla_norm_w, pool_w, pool_scale, w_br_pool, w_br_gla, w_out,
              ffn2_up, ffn2_down, final_norm_w):
    B = x.shape[0]
    zero_state = jnp.zeros((B, GLA_HEADS, GLA_DK, GLA_DV), jnp.float32)
    for l in range(DEPTH):
        last = l == DEPTH - 1
        lp = {
            'w_in': w_in[l], 'w_af_up': w_af_up[l], 'b_af': b_af[l], 'w_ab_up': w_ab_up[l],
            'b_ab': b_ab[l], 'gla_norm_w': gla_norm_w[l], 'pool_w': pool_w[l],
            'pool_scale': pool_scale[l], 'w_br_pool': w_br_pool[l], 'w_br_gla': w_br_gla[l],
            'w_out': w_out[l],
        }
        nw = norm_w[l]
        sh1, sc1, g1, sh2, sc2, g2, sh3, sc3, g3 = modulation(c[:, None, :], w_mod[l], b_mod[l])
        ch1, cs1, cg1, ch2, cs2, cg2, ch3, cs3, cg3 = modulation(c_ctx[None, None, :], w_mod[l], b_mod[l])

        x = x + 0.5 * g1 * swiglu(modulate(x, nw[0], sh1, sc1), ffn1_up[l], ffn1_down[l])
        ctx = ctx + 0.5 * cg1 * swiglu(modulate(ctx, nw[0], ch1, cs1), ffn1_up[l], ffn1_down[l])

        hc = modulate(ctx, nw[1], ch2, cs2)
        if last:
            s_f, s_b = context_states(hc @ w_in[l][:, :OFF_Q], lp)
        else:
            yc, projc = token_mixer(hc, False, zero_state, zero_state, lp)
            s_f, s_b = context_states(projc, lp)
            ctx = ctx + cg2 * yc
            ctx = ctx + 0.5 * cg3 * swiglu(modulate(ctx, nw[2], ch3, cs3), ffn2_up[l], ffn2_down[l])

        yx, _ = token_mixer(modulate(x, nw[1], sh2, sc2), True, s_f, s_b, lp)
        x = x + g2 * yx

        x = x + 0.5 * g3 * swiglu(modulate(x, nw[2], sh3, sc3), ffn2_up[l], ffn2_down[l])
    return rmsnorm(x, final_norm_w)


_drawn_inputs = setup_inputs


def setup_inputs(seed=0):
    import zlib

    import numpy as np

    out = dict(_drawn_inputs(seed))
    spreads = {}
    factors = {'b_af': 3.124, 'b_ab': 3.597, 'gla_norm_w': 8.0, 'pool_scale': 6.014, 'final_norm_w': 2.82}
    for name, (base, spread) in spreads.items():
        noise = np.random.default_rng([zlib.crc32(name.encode()), seed]).standard_normal(out[name].shape)
        drawn = base * np.exp(spread * noise) if base else spread * noise
        out[name] = __import__('jax').numpy.asarray(drawn.astype(out[name].dtype))
    for name, factor in factors.items():
        out[name] = (out[name] * factor).astype(out[name].dtype)
    return out
```

```python
from contextlib import ExitStack

import numpy as np

import concourse.bass as bass
from concourse import mybir

P = 128
D = 1024
SEQ = 512
CTX = 256
NT = SEQ + CTX
DEPTH = 2
GRID_W = 64
GRID_H = SEQ // GRID_W
WINDOWS = (2, 4, 8, 16)
HEADS = 4
DK = 64
DV = 128
KW = HEADS * DK
VW = HEADS * DV
RANK = 16
TAU = 16.0
CHUNK = 64
D_FF = 2816
N_MOD = 9
EPS = 1e-6
POOLW = 512
OFF_K = 0
OFF_V = OFF_K + KW
OFF_AF = OFF_V + VW
OFF_Q = OFF_AF + 2 * RANK
OFF_R = OFF_Q + KW
OFF_POOL = OFF_R + VW
OFF_GP = OFF_POOL + POOLW
OFF_GG = OFF_GP + D

DC = D // P
NCH = NT // CHUNK
NBLK = NT // P
XBLK = SEQ // P
MODC = N_MOD * DC
MODJ = MODC // 2
START_JOBS = 2 * DC // 2
THIRDS = ((0, 8), (8, 8), (16, 6))
POOL_REC = GRID_H + CTX

F32 = mybir.dt.float32
F32R = mybir.dt.float32r
U8 = mybir.dt.uint8
ALU = mybir.AluOpType
ACT = mybir.ActivationFunctionType
ds = bass.ds

ROW_BMOD, ROW_NORM = 0, MODC
ROW_BAF = ROW_NORM + 3 * DC
ROW_BAB = ROW_BAF + 2
ROW_GN = ROW_BAB + 2
ROW_PS = ROW_GN + 1
ROW_X1 = ROW_PS + 4
ROW_X2 = ROW_X1 + DC
ROWS = (ROW_X2 + DC, ROW_X2)

BOTH = ((0, SEQ), (SEQ, CTX))
LATENT = ((0, SEQ),)


def make_plan():
    plan, unit, pair, job = [], 0, 0, START_JOBS

    def add(kind, layer, pairs, ffn=0, third=0, jobs=0, units=None):
        nonlocal unit, pair, job
        units = 2 * pairs if units is None else units
        plan.append(dict(kind=kind, layer=layer, ffn=ffn, third=third, unit=unit, pair=pair,
                         pairs=pairs, units=units, job=job, jobs=jobs))
        unit, pair, job = unit + units, pair + pairs, job + jobs

    def add_ffn(layer, ffn, jobs):
        for t, (_, n) in enumerate(THIRDS):
            add("up", layer, n, ffn, t, jobs[2 * t])
            add("down", layer, DC // 2, ffn, t, jobs[2 * t + 1])

    left = DEPTH * MODJ - START_JOBS
    slots = [n for _, k in THIRDS for n in (k, DC // 2)]
    for layer in range(DEPTH):
        for ffn in range(2):
            first = layer == 0 and ffn == 0
            if ffn == 1:
                add("proj", layer, 9, units=17)
                add("gates", layer, 2 * DC)
                add("out", layer, DC // 2)
            jobs = []
            for s, n in enumerate(slots):
                room = n if not first else (n, 4, 8, 4, 4, 4)[s]
                take = min(room, left)
                jobs.append(take)
                left -= take
            add_ffn(layer, ffn, jobs)
    assert left == 0
    return plan


def proj_pairs():
    two = lambda what, off, i: [(what, off + (2 * i + s) * P, P, 2 * i + s) for s in range(2)]
    return [[("a", OFF_AF, 2 * RANK, 0)], two("k", OFF_K, 0), two("q", OFF_Q, 0),
            two("u", OFF_POOL, 0), two("u", OFF_POOL, 1), two("v", OFF_V, 0), two("r", OFF_R, 0),
            two("v", OFF_V, 1), two("r", OFF_R, 1)]


PROJ_JOBS = {1: [("z", 0)], 2: [("z", 1)], 3: [("z", 2)], 4: [("z", 3)],
             6: [("vt", 0), ("vt", 1)], 8: [("vt", 2), ("vt", 3)] + [("pw", g) for g in range(4)]}
MISC = 12
FWD = [*range(SEQ // CHUNK, NCH), *range(SEQ // CHUNK)]
BWD = [*range(NCH - 1, SEQ // CHUNK - 1, -1), *range(SEQ // CHUNK - 1, -1, -1)]


def parts_of(kind, layer, what=None):
    if layer == DEPTH - 1 and (kind in ("gates", "out") or what in ("q", "r", "u")):
        return LATENT
    return BOTH


def phase_parts(ph):
    if ph["layer"] == DEPTH - 1 and ph["ffn"] == 1 and ph["kind"] in ("up", "down"):
        return LATENT
    return parts_of(ph["kind"], ph["layer"])


def build(nc, t):
    plan = make_plan()
    ctx = ExitStack()

    def sem(name):
        return ctx.enter_context(nc.semaphore(name))

    def sb(name, shape, dt=F32):
        return ctx.enter_context(nc.sbuf_tensor(name, shape, dt))

    x = sb("x", [P, DC * NT])
    wraw = sb("wraw", [P, 4, DC, P])
    whi = sb("whi", [P, 2, DC, P], F32R)
    wlo = sb("wlo", [P, 2, DC, P], F32R)
    modv = sb("modv", [P, 2 * DEPTH * MODC])
    vecs = sb("vecs", [P, 2, P])
    ident = sb("ident", [P, P])
    ones = sb("ones", [P, P])
    masks = sb("masks", [P, 2, 2 * P], U8)
    gate = sb("gate", [P, 2 * DC])
    amul = sb("amul", [P, 2 * DC])
    cond = sb("cond", [P, 2 * DC])
    eps = sb("eps", [P, 1])
    rstd = sb("rstd", [P, NT])

    class Layout:

        def __init__(self):
            self.stack, self.n = ExitStack(), 0

        def __call__(self, name, shape, dt=F32):
            return self.stack.enter_context(nc.sbuf_tensor(name, shape, dt))

        def skip(self, kib, name):
            return self(name, [P, kib * 256])

        def done(self):
            self.stack.close()

    lay = Layout()
    hhi = lay("hhi", [P, DC * NT], F32R)
    hlo = lay("hlo", [P, DC * NT], F32R)
    mhi = lay("mhi", [P, DC * NT], F32R)
    mlo = lay("mlo", [P, DC * NT], F32R)
    yphi = lay("yphi", [P, 4 * NT], F32R)
    yplo = lay("yplo", [P, 4 * NT], F32R)
    yghi = lay("yghi", [P, 4 * NT], F32R)
    yglo = lay("yglo", [P, 4 * NT], F32R)
    lay.done()

    lay = Layout()
    lay.skip(48, "pad_start")
    xrow = lay("xrow", [P, NBLK, D])
    vrow = lay("vrow", [P, 2, P])
    mrow = lay("mrow", [P, 4 * P])
    lay.done()

    lay = Layout()
    lay.skip(96, "pad_ffn")
    ssq = lay("ssq", [P, NT])
    sq = lay("sq", [P, 2, NT])
    htmp = lay("htmp", [P, 2, NT])
    stmp = lay("stmp", [P, 2, NT])
    mtmp = lay("mtmp", [P, 2, NT])
    modraw = lay("modraw", [P, 2, DC, 2 * P])
    macc = lay("macc", [P, 2, 2, 2 * P])
    lay.done()

    lay = Layout()
    lay.skip(48, "pad_proj")
    kq = lay("kq", [P, 4, NT])
    vt = lay("vt", [P, NBLK, VW])
    rsil = lay("rsil", [P, 4, NT])
    bsum = lay("bsum", [P, 4, NT])
    vf = lay("vf", [P, 2, NT])
    z = lay("z", [P, 3, NT])
    reset = lay("reset", [P, NT])
    alow = lay("alow", [P, NT])
    wup = lay("wup", [P, 2, KW])
    lay.skip(1, "pad_proj2")
    u = lay("u", [P, 4, NT])
    racc = lay("racc", [P, SEQ])
    cacc = lay("cacc", [P, NT])
    poolw = lay("poolw", [P, 4, P])
    recs = lay("recs", [P, 4, POOL_REC])
    lay.done()

    lay = Layout()
    qbd = lay("qbd", [P, 2, 2, NT])
    kt = lay("kt", [P, 2, NT])
    kpad = lay("kpad", [P, 2, NBLK, 2, P])
    states = lay("states", [P, 2, NCH, DV])
    lay.skip(6, "pad_gla")
    lay.skip(48 + 24, "pad_gla2")
    ex = lay("ex", [P, 2, 3, NT])
    att = lay("att", [P, 2, 2 * P])
    dec = lay("dec", [P, 2, NCH])
    lay.done()

    lay = Layout()
    osq = lay("osq", [P, 2, NT])
    orstd = lay("orstd", [P, 4, NT])
    oy = lay("oy", [P, 2, NT])
    lay.done()

    lay = Layout()
    lay.skip(48, "pad_merge")
    mf = lay("mf", [P, 2, DC * NT])
    lay.done()

    lay = Layout()
    lay.skip(48, "pad_end")
    orow = lay("orow", [P, XBLK, D])
    lay.done()

    ps = ctx.enter_context(nc.psum_tensor("ps", [P, 8 * 512], F32))

    def bank(b, c0=0, n=512):
        return ps[:, 512 * b + c0:512 * b + c0 + n]

    def pair_ps(b, s, part, rows=P):
        t0, n = part
        c = 512 * (3 * b + s) if t0 == 0 else 512 * (3 * b + 2) + CTX * s
        return ps[0:rows, c:c + n]

    w_loaded = [sem(f"w_loaded{i}") for i in range(4)]
    hi_split = sem("hi_split")
    lo_split = sem("lo_split")
    w_used = sem("w_used")
    pair_free = sem("pair_free")
    silu_done = sem("silu_done")
    mhi_done = sem("mhi_done")
    m_ready = sem("m_ready")
    s_const = sem("s_const")
    s_x = [sem(f"x_landed{i}") for i in range(2)]
    s_rows = sem("s_rows")
    s_mix = sem("s_mix")
    set_up = sem("set_up")
    vec_t = sem("vec_t")
    vec_ready = sem("vec_ready")
    cond_ready = sem("cond_ready")
    xt_ready = sem("xt_ready")
    xt_used = sem("xt_used")
    mod_loaded = [sem(f"mod_loaded{i}") for i in range(2)]
    mod_step = sem("mod_step")
    mod_sum = sem("mod_sum")
    mod_done = sem("mod_done")
    sq_ready = sem("sq_ready")
    sq_used = sem("sq_used")
    var_ready = sem("var_ready")
    std_ready = sem("std_ready")
    ht_ready = sem("ht_ready")
    hhi_ready = sem("hhi_ready")
    h_ready = sem("h_ready")
    pooled = sem("pooled")
    misc_ready = sem("misc_ready")
    misc_free = sem("misc_free")
    z_abs = sem("z_abs")
    z_log = sem("z_log")
    yp_hi = sem("yp_hi")
    b_ready = sem("b_ready")
    gla_zero = sem("gla_zero")
    d_ready = sem("d_ready")
    e_ready = sem("e_ready")
    prep_ready = sem("prep_ready")
    kend_t = sem("kend_t")
    kpad_ready = sem("kpad_ready")
    kv_ready = sem("kv_ready")
    kv_used = sem("kv_used")
    s_ready = sem("s_ready")
    att_ready = sem("att_ready")
    o_ready = sem("o_ready")
    o_used = sem("o_used")
    osq_ready = sem("osq_ready")
    ovar_ready = sem("ovar_ready")
    ostd_ready = sem("ostd_ready")
    oy_ready = sem("oy_ready")
    yghi_ready = sem("yghi_ready")
    yg_ready = sem("yg_ready")
    merge_ready = sem("merge_ready")
    out_t = sem("out_t")
    out_row = sem("out_row")
    stored = sem("stored")
    pool_step = sem("pool_step")
    dve_step = sem("dve_step")
    act_step = sem("act_step")

    def repeat(eng, start, end, first, body):
        if first and start < end:
            body(start)
            start += 1
        if end - start == 1:
            body(start)
        elif end > start:
            with eng.Fori(start, end) as i:
                body(i)

    def segments(ph):
        if ph is plan[-1]:
            return [(a, a + 1, False) for a in range(ph["pairs"] // 2)]
        j = ph["jobs"] // 2
        return [(a, b, w) for a, b, w in ((0, j, True), (j, ph["pairs"] // 2, False)) if a < b]

    def at_least(eng, s, value):
        if not isinstance(value, int) or value > 0:
            eng.wait_ge(s, value)

    class Steps:

        def __init__(self, eng, s):
            self.eng, self.s, self.n = eng, s, 0

        def link(self, ins):
            self.n += 1
            ins.then_inc(self.s, 1)
            self.eng.wait_ge(self.s, self.n)

    def last_norm_out(ph):
        return (ph["kind"] == "down" and ph["third"] == 2) or ph["kind"] == "out"

    norm_of = {}
    for n_, ph_ in enumerate([p for p in plan if last_norm_out(p)]):
        norm_of[(ph_["layer"], ph_["kind"], ph_["ffn"])] = n_ + 1

    def m_base(l, ffn, third=0):
        hidden = sum(n for _, n in THIRDS)
        return hidden * (2 * l + ffn) + DC * (l + ffn) + sum(n for _, n in THIRDS[:third])

    def m_base_merge(l):
        return m_base(l, 1) - DC

    def proj_tensor(pe, l, u0, p0, unit_products):
        unit, misc = u0, MISC * l
        for n, units in enumerate(proj_pairs()):
            pair = p0 + n
            pe.wait_ge(pair_free, pair - 1)
            for s, (what, _, _, _) in enumerate(units):
                outs = [(pt, pair_ps(pair % 2, s, pt)) for pt in parts_of("proj", l, what)]
                wait = (h_ready, DC * (4 * l + 1) + 1) if n == 0 else None
                mm = unit_products(unit, unit % 2, DC, hhi, hlo, outs, wait)
                mm.then_inc(w_used, 1)
                unit += 1
            for job, g in PROJ_JOBS.get(n, []):
                at_least(pe, misc_free, misc)
                if job == "z":
                    pr, d = g // 2, g % 2
                    pe.wait_ge(pair_free, p0 + 1)
                    pe.wait_ge(s_mix, 16 * 5 * (l + 1))
                    for t0, c in BOTH:
                        mm = nc.tensor.matmul(ps[:, 3072 + t0:3072 + t0 + c],
                                              wup[0:2 * RANK, d, pr * P:(pr + 1) * P],
                                              alow[0:2 * RANK, t0:t0 + c], start=True, stop=True)
                elif job == "vt":
                    pe.wait_ge(pair_free, p0 + (6, 8)[g // 2])
                    for b in range(NBLK):
                        mm = nc.tensor.transpose(bank(6, b * P, P), vf[:, g % 2, b * P:(b + 1) * P], ident[:])
                else:
                    pe.wait_ge(pooled, 4 * l + g + 1)
                    for t0, c in parts_of("proj", l, "u"):
                        mm = nc.tensor.matmul(ps[:, 3072 + t0:3072 + t0 + c], poolw[:, g, :],
                                              u[:, g, t0:t0 + c], start=True, stop=True)
                mm.then_inc(misc_ready, 1)
                misc += 1

    def blocks(l):
        return NBLK if l < DEPTH - 1 else XBLK

    def o_before(l, pr):
        return 2 * sum(blocks(i) for i in range(l)) + pr * blocks(l)

    KV_STEPS = NCH - 1

    def gla_tensor(pe, l, p0):
        pe.wait_ge(pair_free, p0 + 9)
        pe.wait_ge(misc_free, MISC * (l + 1))
        for pr in range(2):
            ob, nb, kv0 = o_before(l, pr), blocks(l), (2 * l + pr) * KV_STEPS
            at_least(pe, o_used, ob)
            for d in range(2):
                pe.wait_ge(prep_ready, 4 * l + 2 * pr + d + 1)
                for b in range(NBLK):
                    mm = nc.tensor.transpose(bank(2 * d, b * P, P), ex[:, d, 2, b * P:(b + 1) * P], ident[:])
                mm.then_inc(kend_t, 1)

            def scores(b):
                at_least(pe, att_ready, ob + b - 1)
                for d in range(2):
                    mm = nc.tensor.matmul(bank(6 + b % 2, d * 2 * P, 2 * P), kt[:, d, b * P:(b + 1) * P],
                                          qbd[:, d, :, b * P:(b + 1) * P], start=True, stop=True)
                mm.then_inc(s_ready, 1)

            pe.wait_ge(kpad_ready, 4 * l + 2 * pr + 2)
            scores(0)
            scores(1)
            for s in range(KV_STEPS):
                at_least(pe, kv_used, kv0 + s - 1)
                for d, order in enumerate((FWD, BWD)):
                    c = order[s]
                    mm = nc.tensor.matmul(bank(4 + s % 2, d * 2 * P, 2 * P), kpad[:, d, c // 2, c % 2, :],
                                          vt[:, c // 2, 2 * pr * DV:2 * (pr + 1) * DV], start=True, stop=True)
                mm.then_inc(kv_ready, 1)
            pe.wait_ge(kv_used, kv0 + KV_STEPS)
            for b in range(nb):
                pe.wait_ge(att_ready, ob + b + 1)
                at_least(pe, o_used, ob + b - 1)
                o = bank(b % 2, 0, 2 * P)
                terms = [(o[:, h * P:(h + 1) * P], vt[:, b, (2 * pr + h) * DV:(2 * pr + h + 1) * DV],
                          att[:, b % 2, h * P:(h + 1) * P]) for h in range(2)]
                for half in range(2):
                    c = 2 * b + half
                    for d, order in enumerate((FWD, BWD)):
                        if c != order[0]:
                            terms.append((o.rearrange("p (h c) -> p h c", h=2)[:, :, half * CHUNK:(half + 1) * CHUNK],
                                          states[:, d, c, :],
                                          qbd[:, d, :, c * CHUNK:(c + 1) * CHUNK]))
                for n, (out, lhsT, rhs) in enumerate(terms):
                    mm = nc.tensor.matmul(out, lhsT, rhs, start=(n == 0), stop=(n == len(terms) - 1),
                                          skip_group_check=True)
                mm.then_inc(o_ready, 1)
                if b + 2 < nb:
                    scores(b + 2)
        pe.wait_ge(o_used, o_before(l + 1, 0))
        for h in range(HEADS):
            pe.wait_ge(osq_ready, 4 * l + h + 1)
            for t0, c in parts_of("gates", l):
                mm = nc.tensor.matmul(ps[:, 1024 * h + t0:1024 * h + t0 + c], ones[:], osq[:, h % 2, t0:t0 + c],
                                      start=True, stop=True)
            mm.then_inc(ovar_ready, 1)
        pe.wait_ge(ostd_ready, 4 * (l + 1))

    def w_load_count(unit, slot4):
        return 4 * unit + (16 - 4 * slot4)

    def proj_scalar(act, steps, l, u0, p0, split_hi):
        unit, misc = u0, MISC * l
        for n, units in enumerate(proj_pairs()):
            for s in range(1, len(units) + 1):
                split_hi(unit + s, (unit + s) % 4, (unit + s) % 2)
            unit += len(units)
            buf, what = (p0 + n) % 2, units[0][0]
            parts = parts_of("proj", l, what)
            if what in "akur":
                act.wait_ge(w_used, unit)
                act.wait_ge(pair_free, p0 + n)
                for s, (_, _, m, idx) in enumerate(units):
                    for pt in parts:
                        t0, c = pt
                        dst = {"a": alow[0:m, t0:t0 + c], "k": kq[:, idx % 4, t0:t0 + c], "u": u[:, idx % 4, t0:t0 + c],
                               "r": rsil[:, idx % 4, t0:t0 + c]}[what]
                        ins = nc.scalar.activation(dst, pair_ps(buf, s, pt, m), ACT.Silu if what == "r" else ACT.Copy)
                ins.then_inc(pair_free, 1)
            for job, g in PROJ_JOBS.get(n, []):
                misc += 1
                if job == "z":
                    pr, d = g // 2, g % 2
                    row = (ROW_BAF, ROW_BAB)[d] + pr
                    act.wait_ge(misc_ready, misc)
                    at_least(act, b_ready, 4 * l + g)
                    nc.scalar.activation(z[:, 0, :], ps[:, 3072:3072 + NT], ACT.Abs,
                                         bias=vecs[:, l, row:row + 1]).then_inc(z_abs, 1)
                    act.wait_ge(z_abs, 4 * l + g + 1)
                    steps.link(nc.scalar.activation(z[:, 0, :], z[:, 0, :], ACT.Exp, scale=-1.0))
                    nc.scalar.activation(z[:, 0, :], z[:, 0, :], ACT.Ln, bias=1.0).then_inc(z_log, 1)
                elif job == "pw":
                    act.wait_ge(misc_ready, misc)
                    act.wait_ge(misc_free, MISC * l + 8)
                    c = sum(pt[1] for pt in parts_of("proj", l, "u"))
                    nc.scalar.activation(yphi[:, g * NT:g * NT + c], ps[:, 3072:3072 + c], ACT.Copy,
                                         scale=vecs[:, l, ROW_PS + g:ROW_PS + g + 1]).then_inc(yp_hi, 1)

    def gla_scalar(act, steps, l):
        for pr in range(2):
            ob, nb = o_before(l, pr), blocks(l)
            for d in range(2):
                b = bsum[:, 2 * pr + d, :]
                end = b.rearrange("p (n c) -> p n c", c=CHUNK)[:, :, (CHUNK - 1, 0)[d]]
                act.wait_ge(d_ready, 4 * l + 2 * pr + d + 1)
                nc.scalar.activation(ex[:, d, 0, :], b, ACT.Exp, scale=1.0 / TAU)
                nc.scalar.activation(ex[:, d, 1, :], b, ACT.Exp, scale=-1.0 / TAU)
                nc.scalar.activation(dec[:, d, :], end, ACT.Exp, scale=1.0 / TAU)
                nc.scalar.activation(ex[:, d, 2, :], ex[:, d, 2, :], ACT.Exp, scale=1.0 / TAU).then_inc(e_ready, 1)
            for d in range(2):
                act.wait_ge(kend_t, 4 * l + 2 * pr + d + 1)
                if pr == 0 and d == 0:
                    act.wait_ge(gla_zero, l + 1)
                src = bank(2 * d, 0, NT).rearrange("p (b n) -> p b n", b=NBLK)
                nc.scalar.activation(kpad[0:CHUNK, d, :, 0, :], src[0:CHUNK], ACT.Copy)
                nc.scalar.activation(kpad[CHUNK:P, d, :, 1, :], src[CHUNK:P], ACT.Copy).then_inc(kpad_ready, 1)
            for b in range(nb):
                act.wait_ge(o_ready, ob + b + 1)
                nc.scalar.activation(bsum[:, 2 * pr:2 * pr + 2, b * P:(b + 1) * P],
                                     bank(b % 2, 0, 2 * P).rearrange("p (h n) -> p h n", h=2),
                                     ACT.Copy).then_inc(o_used, 1)
        act.wait_ge(o_used, o_before(l + 1, 0))
        c = sum(pt[1] for pt in parts_of("gates", l))
        for h in range(HEADS):
            at_least(act, ovar_ready, 4 * l + h - 1)
            nc.scalar.activation(osq[:, h % 2, 0:c], bsum[:, h, 0:c], ACT.Square).then_inc(osq_ready, 1)
        for h in range(HEADS):
            act.wait_ge(ovar_ready, 4 * l + h + 1)
            nc.scalar.activation(orstd[:, h, 0:c], ps[:, 1024 * h:1024 * h + c], ACT.Sqrt, bias=eps[:, 0:1],
                                 scale=1.0 / DV).then_inc(ostd_ready, 1)
        for h in range(HEADS):
            act.wait_ge(oy_ready, 4 * l + h + 1)
            nc.scalar.activation(yghi[:, h * NT:h * NT + c], oy[:, h % 2, 0:c], ACT.Copy).then_inc(yghi_ready, 1)

    def mod_needed(l, blocks_of_d):
        return l * MODJ + blocks_of_d * DC // 2

    def proj_vector(dve, steps, l, u0, p0, split_lo):
        nc.vector.memset(wup[:], 0.0).then_inc(set_up, 1)
        unit, misc = u0, MISC * l
        for n, units in enumerate(proj_pairs()):
            for s in range(1, len(units) + 1):
                split_lo(unit + s, (unit + s) % 4, (unit + s) % 2)
            unit += len(units)
            buf, what = (p0 + n) % 2, units[0][0]
            if what in "qv":
                dve.wait_ge(w_used, unit)
                dve.wait_ge(pair_free, p0 + n)
                if what == "v":
                    at_least(dve, misc_ready, MISC * l + 4 + units[0][3])
                for s, (_, _, m, idx) in enumerate(units):
                    for pt in parts_of("proj", l, what):
                        t0, c = pt
                        dst = kq[:, 2 + idx % 2, t0:t0 + c] if what == "q" else vf[:, s, t0:t0 + c]
                        ins = nc.vector.tensor_scalar(dst, pair_ps(buf, s, pt), DK ** -0.5 if what == "q" else 1.0,
                                                      None, ALU.mult)
                ins.then_inc(pair_free, 1)
            for job, g in PROJ_JOBS.get(n, []):
                misc += 1
                if job == "z":
                    pr, d = g // 2, g % 2
                    row = (ROW_BAF, ROW_BAB)[d] + pr
                    dve.wait_ge(z_abs, 4 * l + g + 1)
                    nc.vector.tensor_scalar(z[:, 1, :], ps[:, 3072:3072 + NT], vecs[:, l, row:row + 1], 0.0,
                                            ALU.add, ALU.min).then_inc(misc_free, 1)
                    dve.wait_ge(z_log, 4 * l + g + 1)
                    dve.wait_ge(misc_free, misc)
                    steps.link(nc.vector.tensor_tensor(z[:, 1, :], z[:, 1, :], z[:, 0, :], ALU.subtract))
                    if g == 0:
                        dve.wait_ge(s_mix, 16 * 5 * (l + 1))
                    if d == 0:
                        nc.vector.tensor_tensor_scan(bsum[:, g, :], reset[:], z[:, 1, :], 0.0, ALU.mult,
                                                     ALU.add).then_inc(b_ready, 1)
                    else:
                        steps.link(nc.vector.tensor_tensor_scan(z[:, 2, :], reset[:], z[:, 1, :], 0.0, ALU.mult, ALU.add))
                        zc = z[:, 2, :].rearrange("p (n c) -> p n c", c=CHUNK)
                        steps.link(nc.vector.tensor_tensor(
                            z[:, 0, :].rearrange("p (n c) -> p n c", c=CHUNK),
                            zc[:, :, CHUNK - 1:CHUNK].to_broadcast([P, NCH, CHUNK]), zc, ALU.subtract))
                        nc.vector.tensor_tensor(bsum[:, g, :], z[:, 0, :], z[:, 1, :], ALU.add).then_inc(b_ready, 1)
                elif job == "vt":
                    dve.wait_ge(misc_ready, misc)
                    nc.vector.tensor_copy(vt[:, :, g * DV:(g + 1) * DV],
                                          bank(6, 0, NT).rearrange("p (b n) -> p b n", b=NBLK)).then_inc(misc_free, 1)
                else:
                    c = sum(pt[1] for pt in parts_of("proj", l, "u"))
                    dve.wait_ge(yp_hi, 4 * l + g + 1)
                    nc.vector.scalar_tensor_tensor(
                        out=yplo[:, g * NT:g * NT + c], in0=ps[:, 3072:3072 + c],
                        scalar=vecs[:, l, ROW_PS + g:ROW_PS + g + 1], in1=yphi[:, g * NT:g * NT + c].bitcast(F32),
                        op0=ALU.mult, op1=ALU.subtract).then_inc(misc_free, 1)

    def gla_vector(dve, steps, l):
        for pr in range(2):
            ob, nb, kv0 = o_before(l, pr), blocks(l), (2 * l + pr) * KV_STEPS
            at_least(dve, kend_t, 4 * l + 2 * pr)
            for d in range(2):
                b = bsum[:, 2 * pr + d, :].rearrange("p (n c) -> p n c", c=CHUNK)
                e = (CHUNK - 1, 0)[d]
                nc.vector.tensor_tensor(ex[:, d, 2, :].rearrange("p (n c) -> p n c", c=CHUNK),
                                        b[:, :, e:e + 1].to_broadcast([P, NCH, CHUNK]), b,
                                        ALU.subtract).then_inc(d_ready, 1)
            at_least(dve, o_ready, ob)
            dve.wait_ge(gla_zero, l + 1)
            xc = SEQ if l == DEPTH - 1 else NT
            for d in range(2):
                dve.wait_ge(e_ready, 4 * l + 2 * pr + d + 1)
                for h in range(2):
                    r = slice(h * DK, (h + 1) * DK)
                    nc.vector.tensor_tensor(qbd[r, d, h, 0:xc], kq[r, 2 + pr, 0:xc], ex[r, d, 0, 0:xc], ALU.mult)
                nc.vector.tensor_tensor(kt[:, d, :], kq[:, pr, :], ex[:, d, 1, :], ALU.mult)
                nc.vector.tensor_tensor(ex[:, d, 2, :], kq[:, pr, :], ex[:, d, 2, :], ALU.mult).then_inc(prep_ready, 1)

            def mask_scores(b):
                dve.wait_ge(s_ready, ob + b + 1)
                at_least(dve, o_ready, ob + b - 1)
                steps.link(nc.vector.copy_predicated(att[:, b % 2, :], masks[:, 0, :], bank(6 + b % 2, 0, 2 * P)))
                nc.vector.copy_predicated(att[:, b % 2, :], masks[:, 1, :],
                                          bank(6 + b % 2, 2 * P, 2 * P)).then_inc(att_ready, 1)

            mask_scores(0)
            mask_scores(1)
            for s in range(KV_STEPS):
                dve.wait_ge(kv_ready, kv0 + s + 1)
                if s:
                    dve.wait_ge(kv_used, kv0 + s)
                for d, order in enumerate((FWD, BWD)):
                    c, nxt = order[s], order[s + 1]
                    for h in range(2):
                        r = slice(h * DK, (h + 1) * DK)
                        kv = ps[r, 512 * (4 + s % 2) + d * 2 * P + h * DV:512 * (4 + s % 2) + d * 2 * P + (h + 1) * DV]
                        if s == 0:
                            ins = nc.vector.tensor_copy(states[r, d, nxt, :], kv)
                        else:
                            ins = nc.vector.scalar_tensor_tensor(
                                out=states[r, d, nxt, :], in0=states[r, d, c, :], scalar=dec[r, d, c:c + 1],
                                in1=kv, op0=ALU.mult, op1=ALU.add)
                ins.then_inc(kv_used, 1)
            for b in range(2, nb):
                mask_scores(b)
        c = sum(pt[1] for pt in parts_of("gates", l))
        for h in range(HEADS):
            dve.wait_ge(ostd_ready, 4 * l + h + 1)
            steps.link(nc.vector.reciprocal(orstd[:, h, 0:c], orstd[:, h, 0:c]))
            at_least(dve, yg_ready, 4 * l + h - 1)
            steps.link(nc.vector.scalar_tensor_tensor(
                out=oy[:, h % 2, 0:c], in0=bsum[:, h, 0:c], scalar=vecs[:, l, ROW_GN:ROW_GN + 1],
                in1=orstd[:, h, 0:c], op0=ALU.mult, op1=ALU.mult))
            nc.vector.tensor_tensor(oy[:, h % 2, 0:c], oy[:, h % 2, 0:c], rsil[:, h, 0:c], ALU.mult).then_inc(oy_ready, 1)
            dve.wait_ge(yghi_ready, 4 * l + h + 1)
            nc.vector.tensor_tensor(yglo[:, h * NT:h * NT + c], oy[:, h % 2, 0:c],
                                    yghi[:, h * NT:h * NT + c].bitcast(F32), ALU.subtract).then_inc(yg_ready, 1)

    with ctx:
        block = ctx.enter_context(nc.Block())

        @block.sync
        def _(sp):
            wm = [t["w_mod"][l].rearrange("(c p) n -> p c n", p=P) for l in range(DEPTH)]

            def load_mod(job, layer, buf):
                at_least(sp, mod_step, DC * 2 * (job - 1))
                sp.dma_start(modraw[:, buf], wm[layer][:, :, ds((job - layer * MODJ) * 2 * P, 2 * P)]
                             ).then_inc(mod_loaded[buf], 16)

            def load_unit(unit, slot, src, k, cols=P):
                at_least(sp, lo_split, unit - 3)
                sp.dma_start(wraw[:, slot, 0:k, 0:cols], src).then_inc(w_loaded[slot], 16)

            for l in range(DEPTH):
                for name, row in (("b_mod", ROW_BMOD), ("norm_w", ROW_NORM), ("b_af", ROW_BAF),
                                  ("b_ab", ROW_BAB), ("gla_norm_w", ROW_GN), ("pool_scale", ROW_PS)):
                    src = t[name][l]
                    src = src.rearrange("a (r q) -> (a r) q", q=P) if len(src.shape) == 2 else \
                        src.rearrange("(r q) -> r q", q=P)
                    sp.dma_start(vrow[row:row + src.shape[0], l, :], src).then_inc(s_rows, 16)
            sp.dma_start(vrow[ROW_X1:ROW_X1 + DC, 0, :], t["c"][0].rearrange("(r q) -> r q", q=P)).then_inc(s_rows, 16)
            sp.dma_start(vrow[ROW_X2:ROW_X2 + DC, 0, :], t["c_ctx"].rearrange("(r q) -> r q", q=P)).then_inc(s_rows, 16)
            sp.dma_start(vrow[ROW_X1:ROW_X1 + DC, 1, :], t["final_norm_w"].rearrange("(r q) -> r q", q=P)).then_inc(s_rows, 16)
            for j in range(START_JOBS):
                load_mod(j, 0, j % 2)

            for ph in plan:
                l, kind, u0, j0 = ph["layer"], ph["kind"], ph["unit"], ph["job"]
                f0, fk = THIRDS[ph["third"]]
                up = t["ffn1_up" if ph["ffn"] == 0 else "ffn2_up"][l].rearrange("(c p) n -> p c n", p=P)
                down = t["ffn1_down" if ph["ffn"] == 0 else "ffn2_down"][l].rearrange("(c p) n -> p c n", p=P)
                w_in = t["w_in"][l].rearrange("(c p) n -> p c n", p=P)
                w_pool = t["w_br_pool"][l].rearrange("(c p) n -> p c n", p=P)
                w_gla = t["w_br_gla"][l].rearrange("(c p) n -> p c n", p=P)
                w_out = t["w_out"][l].rearrange("(c p) n -> p c n", p=P)
                if kind == "proj":
                    unit = u0
                    todo = [w for pair in proj_pairs() for w in pair]
                    for _, col, m, _ in todo[:3]:
                        load_unit(unit, unit % 4, w_in[:, :, col:col + m], DC, m)
                        unit += 1
                    sp.wait_ge(h_ready, DC * (4 * l + 2))
                    sp.dma_start(reset[:], t["const_reset"].partition_broadcast(P)).then_inc(s_mix, 16)
                    sp.dma_start(poolw[:], t["pool_w"][l].rearrange("g p q -> p g q")).then_inc(s_mix, 16)
                    sp.dma_start(recs[:], t["const_pool"].partition_broadcast(P)).then_inc(s_mix, 16)
                    sp.wait_ge(set_up, 2 + l)
                    sp.dma_start(wup[0:RANK, 0, :], t["w_af_up"][l]).then_inc(s_mix, 16)
                    sp.dma_start(wup[RANK:2 * RANK, 1, :], t["w_ab_up"][l]).then_inc(s_mix, 16)
                    for _, col, m, _ in todo[3:]:
                        load_unit(unit, unit % 4, w_in[:, :, col:col + m], DC, m)
                        unit += 1
                    continue
                for a, b, jobs in segments(ph):
                    def body(i, jobs=jobs):
                        nxt = sp.snap((i + 1) * P) if kind == "gates" else 0
                        for h in range(2):
                            for s in range(2):
                                unit = u0 + 4 * i + 2 * h + s
                                slot = (u0 + 2 * h + s) % 4
                                if kind == "up":
                                    src, k = up[:, :, ds((f0 + 2 * i + h) * P + s * D_FF, P)], DC
                                elif kind == "down":
                                    src, k = down[:, f0:f0 + fk, ds((4 * i + 2 * h + s) * P, P)], fk
                                elif kind == "out":
                                    src, k = w_out[:, :, ds((4 * i + 2 * h + s) * P, P)], DC
                                elif h == 0:
                                    src, k = w_in[:, :, ds(OFF_GP + s * D - P + nxt, P)], DC
                                else:
                                    src, k = (w_pool, w_gla)[s][:, :, ds(nxt - P, P)], 4
                                load_unit(unit, slot, src, k)
                            if jobs:
                                load_mod(j0 + 2 * i + h, (j0 >= MODJ) * 1, (j0 + h) % 2)
                    repeat(sp, a, b, u0 == 0 and a == 0, body)

            sp.wait_ge(out_row, DC)
            for b in range(XBLK):
                sp.dma_start(t["out"][0, b * P:(b + 1) * P, :], orow[:, b, :]).then_inc(stored, 16)
            sp.wait_ge(stored, 16 * XBLK)

        @block.tensor
        def _(pe):
            def unit_products(unit, slot, kk, hi, lo, outs, chunk_wait):
                pe.wait_ge(lo_split, unit + 1)
                for k in range(kk):
                    if chunk_wait is not None:
                        pe.wait_ge(chunk_wait[0], chunk_wait[1] + k)
                    for w, a in ((whi, hi), (whi, lo), (wlo, hi)):
                        for (t0, n), o in outs:
                            last = k == kk - 1 and w is wlo
                            mm = nc.tensor.matmul(o, w[:, slot, k, :], a[:, k * NT + t0:k * NT + t0 + n],
                                                  start=(k == 0 and w is whi and a is hi), stop=last)
                return mm

            def norm_sum(n, parts):
                pe.wait_ge(sq_used, DC * (n + 1))
                if n == 0:
                    pe.wait_ge(set_up, 1)
                pe.wait_ge(mod_done, min([p["job"] + p["jobs"] for p in plan if last_norm_out(p)][n - 1]
                                         if n else START_JOBS, DEPTH * MODJ))
                for t0, c in parts:
                    mm = nc.tensor.matmul(ps[:, 6 * 512 + t0:6 * 512 + t0 + c], ones[:], ssq[:, t0:t0 + c],
                                          start=True, stop=True)
                mm.then_inc(var_ready, 1)

            def mod_sums(job, buf):
                pe.wait_ge(mod_step, DC * 2 * (job + 1))
                for c in range(2):
                    for h in range(2):
                        mm = nc.tensor.matmul(bank(6, 2 * c + h, 1), macc[:, buf, c, h * P:(h + 1) * P],
                                              ones[:, 0:1], start=True, stop=True)
                mm.then_inc(mod_sum, 1)

            pe.wait_ge(s_const, 32)
            pe.wait_ge(s_rows, 16 * 15)
            for l in range(DEPTH):
                mm = nc.tensor.transpose(bank(7, l * P, ROWS[l]), vrow[0:ROWS[l], l, :], ident[0:ROWS[l], 0:ROWS[l]])
            mm.then_inc(vec_t, 1)
            for q in s_x:
                pe.wait_ge(q, 16)
            for j in range(DC):
                at_least(pe, xt_used, j - 2)
                for b in range(NBLK):
                    mm = nc.tensor.transpose(bank(2 * (j % 3), b * P, P), xrow[:, b, j * P:(j + 1) * P], ident[:])
                mm.then_inc(xt_ready, 1)
            pe.wait_ge(set_up, 1)
            for j in range(START_JOBS):
                if j:
                    pe.wait_ge(mod_done, j)
                mod_sums(j, j % 2)
            norm_sum(0, BOTH)
            pe.wait_ge(xt_used, DC)

            for n_ph, ph in enumerate(plan):
                l, kind, u0, p0, j0 = ph["layer"], ph["kind"], ph["unit"], ph["pair"], ph["job"]
                fk = THIRDS[ph["third"]][1]
                parts = phase_parts(ph)
                if kind == "proj":
                    proj_tensor(pe, l, u0, p0, unit_products)
                    gla_tensor(pe, l, p0)
                    continue
                if kind in ("up", "down"):
                    m_before = m_base(l, ph["ffn"], ph["third"])
                for a, b, jobs in segments(ph):
                    def body(i, jobs=jobs):
                        for h in range(2):
                            pair, buf = p0 + 2 * i + h, (p0 + h) % 2
                            at_least(pe, pair_free, pair - 1)
                            for s in range(2):
                                unit, slot = u0 + 4 * i + 2 * h + s, (u0 + s) % 2
                                outs = [(pt, pair_ps(buf, s, pt)) for pt in parts]
                                first = h == 0 and s == 0
                                if kind == "up":
                                    wait = (h_ready, DC * (4 * l + 3 * ph["ffn"]) + 1) if first else None
                                    mm = unit_products(unit, slot, DC, hhi, hlo, outs, wait)
                                elif kind == "down":
                                    wait = (m_ready, m_before + 1) if first else None
                                    mm = unit_products(unit, slot, fk, mhi, mlo, outs, wait)
                                elif kind == "out":
                                    wait = (m_ready, m_base_merge(l) + 1) if first else None
                                    mm = unit_products(unit, slot, DC, mhi, mlo, outs, wait)
                                elif h == 0:
                                    wait = (h_ready, DC * (4 * l + 2) + 1) if first else None
                                    mm = unit_products(unit, slot, DC, hhi, hlo, outs, wait)
                                else:
                                    if s == 1:
                                        pe.wait_ge(yg_ready, 4 * (l + 1))
                                    mm = unit_products(unit, slot, 4, (yphi, yghi)[s], (yplo, yglo)[s], outs, None)
                                mm.then_inc(w_used, 1)
                            if jobs:
                                mod_sums(j0 + 2 * i + h, (j0 + h) % 2)
                    repeat(pe, a, b, u0 == 0 and a == 0, body)
                if last_norm_out(ph):
                    n = norm_of[(l, kind, ph["ffn"])]
                    last = n == 3 * DEPTH
                    norm_sum(n, phase_parts(plan[n_ph + 1]) if not last else LATENT)

            for j in range(DC):
                pe.wait_ge(ht_ready, DC * 4 * DEPTH + j + 1)
                at_least(pe, out_row, j - 1)
                for b in range(XBLK):
                    mm = nc.tensor.transpose(bank(j % 2, b * P, P), htmp[:, j % 2, b * P:(b + 1) * P], ident[:])
                mm.then_inc(out_t, 1)

        @block.scalar
        def _(act):
            steps = Steps(act, act_step)

            def split_hi(unit, slot4, slot2):
                act.wait_ge(w_loaded[slot4], w_load_count(unit, slot4))
                at_least(act, w_used, unit - 1)
                nc.scalar.activation(whi[:, slot2], wraw[:, slot4], ACT.Copy).then_inc(hi_split, 1)

            def squares(n, j, parts):
                k = DC * n + j
                at_least(act, sq_used, k - 1)
                c = sum(pt[1] for pt in parts)
                nc.scalar.activation(sq[:, (j if isinstance(j, int) else 0) % 2, 0:c], x[:, ds(j * NT, c)],
                                     ACT.Square).then_inc(sq_ready, 1)

            def norm_apply(a, n, l, which, parts, tmp, new=True):
                if new:
                    act.wait_ge(var_ready, n + 1)
                    c = sum(pt[1] for pt in parts)
                    nc.scalar.activation(rstd[:, 0:c], ps[:, 3072:3072 + c], ACT.Sqrt, bias=eps[:, 0:1],
                                         scale=1.0 / D).then_inc(std_ready, 1)
                for j in range(DC):
                    act.wait_ge(ht_ready, DC * a + j + 1)
                    for c, (t0, m) in enumerate(parts):
                        sh = c * DEPTH * MODC + l * MODC + 3 * which * DC + j
                        ins = nc.scalar.activation(hhi[:, j * NT + t0:j * NT + t0 + m], tmp(j)[:, t0:t0 + m],
                                                   ACT.Identity, bias=modv[:, sh:sh + 1])
                    ins.then_inc(hhi_ready, 1)

            act.dma_start(ident[:], t["const_ident"]).then_inc(s_const, 16)
            act.dma_start(xrow[:, 0:XBLK, :], t["x"][0].rearrange("(b p) n -> p b n", p=P)).then_inc(s_x[0], 16)
            act.dma_start(xrow[:, XBLK:NBLK, :], t["ctx"][0].rearrange("(b p) n -> p b n", p=P)).then_inc(s_x[1], 16)
            act.dma_start(mrow[:], t["const_mask"]).then_inc(s_const, 16)
            act.wait_ge(vec_ready, 1)
            for c in range(2):
                ins = nc.scalar.activation(cond[:, c * DC:(c + 1) * DC], vecs[:, 0, ROW_X1 + c * DC:ROW_X1 + (c + 1) * DC],
                                           ACT.Silu)
            ins.then_inc(cond_ready, 1)
            for j in range(DC):
                act.wait_ge(xt_ready, j + 1)
                nc.scalar.activation(x[:, j * NT:(j + 1) * NT], bank(2 * (j % 3), 0, NT), ACT.Copy).then_inc(xt_used, 1)
                act.wait_ge(xt_used, j + 1)
                squares(0, j, BOTH)
            split_hi(0, 0, 0)
            act.wait_ge(set_up, 1)
            norm_apply(0, 0, 0, 0, BOTH, lambda j: htmp[:, j % 2])

            for n_ph, ph in enumerate(plan):
                l, kind, u0, p0 = ph["layer"], ph["kind"], ph["unit"], ph["pair"]
                parts = phase_parts(ph)
                c = sum(pt[1] for pt in parts)
                if kind == "proj":
                    proj_scalar(act, steps, l, u0, p0, split_hi)
                    gla_scalar(act, steps, l)
                    norm_apply(4 * l + 2, None, l, 1, parts_of("gates", l), lambda j: mf[:, 0, (j % 2) * NT:(j % 2 + 1) * NT], new=False)
                    continue
                for a, b, jobs in segments(ph):
                    def body(i, jobs=jobs):
                        for h in range(2):
                            pair, buf = p0 + 2 * i + h, (p0 + h) % 2
                            unit = u0 + 4 * i + 2 * h
                            for s in range(1, 3):
                                if not (isinstance(i, int) and ph is plan[-1] and 2 * i + h == ph["pairs"] - 1 and s == 2):
                                    split_hi(unit + s, (u0 + 2 * h + s) % 4, (u0 + s) % 2)
                            if kind == "up":
                                act.wait_ge(w_used, unit + 2)
                                for pt in parts:
                                    ins = nc.scalar.activation(stmp[:, h, pt[0]:pt[0] + pt[1]], pair_ps(buf, 0, pt), ACT.Silu)
                                ins.then_inc(silu_done, 1)
                                act.wait_ge(pair_free, pair + 1)
                                nc.scalar.activation(mhi[:, ds((2 * i + h) * NT, c)], mtmp[:, h, 0:c],
                                                     ACT.Copy).then_inc(mhi_done, 1)
                            elif kind == "gates" and h == 0:
                                act.wait_ge(w_used, unit + 2)
                                act.wait_ge(pair_free, pair)
                                for s in range(2):
                                    for pt in parts:
                                        ins = nc.scalar.activation(mf[:, s, ds(i * NT + pt[0], pt[1])],
                                                                   pair_ps(buf, s, pt), ACT.Sigmoid)
                                ins.then_inc(pair_free, 1)
                            elif kind == "gates":
                                act.wait_ge(merge_ready, DC * l + i + 1)
                                col = act.snap((i + 1) * NT)
                                nc.scalar.activation(mhi[:, ds(col - NT, c)], mf[:, 1, ds(col - NT, c)],
                                                     ACT.Copy).then_inc(mhi_done, 1)
                            elif last_norm_out(ph):
                                n = norm_of[(l, kind, ph["ffn"])]
                                for s in range(2):
                                    k = DC * (n - 1) + 4 * i + 2 * h + s
                                    act.wait_ge(pair_free, pair + 1)
                                    act.wait_ge(sq_used, k - 1 + DC)
                                    nc.scalar.activation(sq[:, s, 0:c], x[:, ds((4 * i + 2 * h + s) * NT, c)],
                                                         ACT.Square).then_inc(sq_ready, 1)
                    repeat(act, a, b, u0 == 0 and a == 0, body)
                if last_norm_out(ph):
                    n = norm_of[(l, kind, ph["ffn"])]
                    if n < 3 * DEPTH:
                        nxt = plan[n_ph + 1]
                        which = {"proj": 1}.get(nxt["kind"], 2 * nxt["ffn"])
                        ap = 4 * nxt["layer"] + (0, 1, 3)[which]
                        norm_apply(ap, n, nxt["layer"], which, phase_parts(nxt), lambda j: htmp[:, j % 2])
                    else:
                        act.wait_ge(var_ready, n + 1)
                        nc.scalar.activation(rstd[:, 0:SEQ], ps[:, 3072:3072 + SEQ], ACT.Sqrt, bias=eps[:, 0:1],
                                             scale=1.0 / D).then_inc(std_ready, 1)
            for j in range(DC):
                act.wait_ge(out_t, j + 1)
                nc.scalar.activation(orow[:, :, j * P:(j + 1) * P], bank(j % 2).rearrange("p (b n) -> p b n", b=XBLK),
                                     ACT.Copy).then_inc(out_row, 1)

        @block.vector
        def _(dve):
            steps = Steps(dve, dve_step)

            def split_lo(unit, slot4, slot2):
                dve.wait_ge(hi_split, unit + 1)
                nc.vector.tensor_tensor(wlo[:, slot2], wraw[:, slot4], whi[:, slot2].bitcast(F32),
                                        ALU.subtract).then_inc(lo_split, 1)

            def mod_accumulate(job, buf, ks):
                if ks[0] == 0:
                    dve.wait_ge(mod_loaded[buf], 8 * job + (16 - 8 * buf))
                    at_least(dve, mod_sum, job - 1)
                for k in ks:
                    for c in range(2):
                        if k == 0:
                            ins = nc.vector.tensor_scalar(macc[:, buf, c, :], modraw[:, buf, 0, :],
                                                          cond[:, c * DC:c * DC + 1], None, ALU.mult)
                        else:
                            dve.wait_ge(mod_step, 2 * DC * job + 2 * k - 1 + c)
                            ins = nc.vector.scalar_tensor_tensor(
                                out=macc[:, buf, c, :], in0=modraw[:, buf, k, :],
                                scalar=cond[:, c * DC + k:c * DC + k + 1], in1=macc[:, buf, c, :],
                                op0=ALU.mult, op1=ALU.add)
                        ins.then_inc(mod_step, 1)

            def mod_finish(job, layer):
                dve.wait_ge(mod_sum, job + 1)
                for c in range(2):
                    ins = nc.vector.tensor_tensor(
                        modv[:, ds(c * DEPTH * MODC + 2 * job, 2)], bank(6, 2 * c, 2),
                        vecs[:, layer, ds(ROW_BMOD + 2 * (job - layer * MODJ), 2)], ALU.add)
                ins.then_inc(mod_done, 1)

            def norm_apply(a, l, which, parts, tmp, new=True):
                c = sum(pt[1] for pt in parts)
                if new:
                    dve.wait_ge(mod_done, mod_needed(l, 3 * which + 2))
                    for e in range(2):
                        sc = e * DEPTH * MODC + l * MODC + (3 * which + 1) * DC
                        steps.link(nc.vector.scalar_tensor_tensor(
                            out=amul[:, e * DC:(e + 1) * DC], in0=modv[:, sc:sc + DC], scalar=1.0,
                            in1=vecs[:, l, ROW_NORM + which * DC:ROW_NORM + (which + 1) * DC],
                            op0=ALU.add, op1=ALU.mult))
                    dve.wait_ge(std_ready, 3 * l + which + 1)
                    steps.link(nc.vector.reciprocal(rstd[:, 0:c], rstd[:, 0:c]))

                def scaled(j):
                    if j >= 2:
                        dve.wait_ge(h_ready, DC * a + j - 1)
                    for e, (t0, m) in enumerate(parts):
                        ins = nc.vector.scalar_tensor_tensor(
                            out=tmp(j)[:, t0:t0 + m], in0=x[:, j * NT + t0:j * NT + t0 + m],
                            scalar=amul[:, e * DC + j:e * DC + j + 1], in1=rstd[:, t0:t0 + m],
                            op0=ALU.mult, op1=ALU.mult)
                    ins.then_inc(ht_ready, 1)

                def rest(j):
                    dve.wait_ge(hhi_ready, DC * a + j + 1)
                    for e, (t0, m) in enumerate(parts):
                        sh = e * DEPTH * MODC + l * MODC + 3 * which * DC + j
                        ins = nc.vector.scalar_tensor_tensor(
                            out=hlo[:, j * NT + t0:j * NT + t0 + m], in0=tmp(j)[:, t0:t0 + m],
                            scalar=modv[:, sh:sh + 1], in1=hhi[:, j * NT + t0:j * NT + t0 + m].bitcast(F32),
                            op0=ALU.add, op1=ALU.subtract)
                    ins.then_inc(h_ready, 1)

                scaled(0)
                for j in range(1, DC):
                    scaled(j)
                    rest(j - 1)
                rest(DC - 1)

            dve.memset(ones[:], 1.0)
            dve.memset(eps[:], EPS).then_inc(set_up, 1)
            dve.wait_ge(vec_t, 1)
            for l in range(DEPTH):
                ins = nc.vector.tensor_copy(vecs[:, l, 0:ROWS[l]], bank(7, l * P, ROWS[l]))
            ins.then_inc(vec_ready, 1)
            dve.wait_ge(cond_ready, 1)
            dve.wait_ge(s_const, 32)
            nc.vector.tensor_copy(masks[:].rearrange("p d n -> p (d n)"), mrow[:])
            for j in range(START_JOBS):
                mod_accumulate(j, j % 2, range(DC))
                mod_finish(j, 0)
            split_lo(0, 0, 0)
            norm_apply(0, 0, 0, BOTH, lambda j: htmp[:, j % 2])

            for n_ph, ph in enumerate(plan):
                l, kind, u0, p0, j0 = ph["layer"], ph["kind"], ph["unit"], ph["pair"], ph["job"]
                parts = phase_parts(ph)
                c = sum(pt[1] for pt in parts)
                if kind == "proj":
                    proj_vector(dve, steps, l, u0, p0, split_lo)
                    gla_vector(dve, steps, l)
                    norm_apply(4 * l + 2, l, 1, parts_of("gates", l), lambda j: mf[:, 0, (j % 2) * NT:(j % 2 + 1) * NT], new=False)
                    continue
                if (kind == "down" and ph["third"] == 0) or kind == "out":
                    w = {"out": 5}.get(kind, 2 + 6 * ph["ffn"])
                    dve.wait_ge(mod_done, mod_needed(l, w + 1))
                    for e in range(2):
                        g0 = e * DEPTH * MODC + l * MODC + w * DC
                        steps.link(nc.vector.tensor_scalar(gate[:, e * DC:(e + 1) * DC], modv[:, g0:g0 + DC],
                                                           1.0 if kind == "out" else 0.5, None, ALU.mult))
                m0 = m_base(l, ph["ffn"], ph["third"])
                s0 = m0 - DC * (l + ph["ffn"])
                for a, b, jobs in segments(ph):
                    def body(i, jobs=jobs):
                        for h in range(2):
                            pair, buf = p0 + 2 * i + h, (p0 + h) % 2
                            unit, job = u0 + 4 * i + 2 * h, j0 + 2 * i + h
                            split_lo(unit + 1, (u0 + 2 * h + 1) % 4, (u0 + 1) % 2)
                            if jobs:
                                mod_accumulate(job, (j0 + h) % 2, range(DC // 2))
                            if not (isinstance(i, int) and ph is plan[-1] and 2 * i + h == ph["pairs"] - 1):
                                split_lo(unit + 2, (u0 + 2 * h + 2) % 4, u0 % 2)
                            if jobs:
                                mod_accumulate(job, (j0 + h) % 2, range(DC // 2, DC))
                            if kind == "up":
                                dve.wait_ge(silu_done, s0 + 2 * i + h + 1)
                                at_least(dve, m_ready, m0 + 2 * i + h - 1)
                                for pt in parts:
                                    ins = nc.vector.tensor_tensor(mtmp[:, h, pt[0]:pt[0] + pt[1]], pair_ps(buf, 1, pt),
                                                                  stmp[:, h, pt[0]:pt[0] + pt[1]], ALU.mult)
                                ins.then_inc(pair_free, 1)
                                dve.wait_ge(mhi_done, m0 + 2 * i + h + 1)
                                nc.vector.tensor_tensor(mlo[:, ds((2 * i + h) * NT, c)], mtmp[:, h, 0:c],
                                                        mhi[:, ds((2 * i + h) * NT, c)].bitcast(F32),
                                                        ALU.subtract).then_inc(m_ready, 1)
                            elif kind in ("down", "out"):
                                dve.wait_ge(w_used, unit + 2)
                                for s in range(2):
                                    n = 4 * i + 2 * h + s
                                    for e, (t0, m) in enumerate(parts):
                                        ins = nc.vector.scalar_tensor_tensor(
                                            out=x[:, ds(n * NT + t0, m)], in0=pair_ps(buf, s, (t0, m)),
                                            scalar=gate[:, ds(e * DC + n, 1)], in1=x[:, ds(n * NT + t0, m)],
                                            op0=ALU.mult, op1=ALU.add)
                                ins.then_inc(pair_free, 1)
                            elif h == 0:
                                pass
                            else:
                                dve.wait_ge(w_used, unit + 2)
                                dve.wait_ge(pair_free, pair)
                                for s in range(2):
                                    for t0, m in parts:
                                        v = mf[:, s, ds(i * NT + t0, m)]
                                        ins = nc.vector.tensor_tensor(v, pair_ps(buf, s, (t0, m)), v, ALU.mult)
                                ins.then_inc(pair_free, 1)
                                dve.wait_ge(pair_free, pair + 1)
                                nc.vector.tensor_tensor(mf[:, 1, ds(i * NT, c)], mf[:, 0, ds(i * NT, c)],
                                                        mf[:, 1, ds(i * NT, c)], ALU.add).then_inc(merge_ready, 1)
                                dve.wait_ge(mhi_done, m_base_merge(l) + i + 1)
                                nc.vector.tensor_tensor(mlo[:, ds(i * NT, c)], mf[:, 1, ds(i * NT, c)],
                                                        mhi[:, ds(i * NT, c)].bitcast(F32),
                                                        ALU.subtract).then_inc(m_ready, 1)
                            if jobs:
                                mod_finish(job, (j0 >= MODJ) * 1)
                    repeat(dve, a, b, u0 == 0 and a == 0, body)
                if last_norm_out(ph):
                    n = norm_of[(l, kind, ph["ffn"])]
                    if n < 3 * DEPTH:
                        nxt = plan[n_ph + 1]
                        which = {"proj": 1}.get(nxt["kind"], 2 * nxt["ffn"])
                        norm_apply(4 * nxt["layer"] + (0, 1, 3)[which], nxt["layer"], which,
                                   phase_parts(nxt), lambda j: htmp[:, j % 2])
            dve.wait_ge(std_ready, 3 * DEPTH + 1)
            steps.link(nc.vector.reciprocal(rstd[:, 0:SEQ], rstd[:, 0:SEQ]))
            for j in range(DC):
                at_least(dve, out_t, j - 1)
                nc.vector.scalar_tensor_tensor(out=htmp[:, j % 2, 0:SEQ], in0=x[:, j * NT:j * NT + SEQ],
                                               scalar=vecs[:, 1, ROW_X1 + j:ROW_X1 + j + 1], in1=rstd[:, 0:SEQ],
                                               op0=ALU.mult, op1=ALU.mult).then_inc(ht_ready, 1)

        @block.gpsimd
        def _(pool):
            steps = Steps(pool, pool_step)

            def add_squares(n, j, buf, parts):
                c = sum(pt[1] for pt in parts)
                pool.wait_ge(sq_ready, DC * n + j + 1)
                at_least(pool, sq_used, DC * n + j)
                nc.gpsimd.tensor_tensor(ssq[:, 0:c], ssq[:, 0:c], sq[:, buf, 0:c], ALU.add).then_inc(sq_used, 1)

            def pool_groups(l, p0):
                pool.wait_ge(s_mix, 16 * 5 * (l + 1))
                for g, w in enumerate(WINDOWS):
                    pool.wait_ge(pair_free, p0 + 4 + g // 2)
                    src = u[:, g, :]
                    shifts = [o for o in range(-(w // 2), w // 2) if o]
                    grid = lambda a: a[:, 0:SEQ].rearrange("p (r c) -> p r c", c=GRID_W)
                    steps.link(nc.gpsimd.tensor_copy(racc[:], src[:, 0:SEQ]))
                    for o in shifts:
                        if abs(o) < GRID_H:
                            a, b = max(0, -o) * GRID_W, (GRID_H - max(0, o)) * GRID_W
                            steps.link(nc.gpsimd.tensor_tensor(racc[:, a:b], racc[:, a:b],
                                                               src[:, a + o * GRID_W:b + o * GRID_W], ALU.add))
                    steps.link(nc.gpsimd.tensor_copy(cacc[:, 0:SEQ], racc[:]))
                    for o in shifts:
                        a, b = max(0, -o), GRID_W - max(0, o)
                        steps.link(nc.gpsimd.tensor_tensor(grid(cacc)[:, :, a:b], grid(cacc)[:, :, a:b],
                                                           grid(racc)[:, :, a + o:b + o], ALU.add))
                    half = GRID_W // 2
                    for q in range(2):
                        v = grid(cacc)[:, :, q * half:(q + 1) * half]
                        c0 = GRID_H + q * (CTX - half)
                        rec = recs[:, g, None, c0:c0 + half].to_broadcast([P, GRID_H, half])
                        steps.link(nc.gpsimd.tensor_tensor(v, v, rec, ALU.mult))
                    rec = recs[:, g, 0:GRID_H, None].to_broadcast([P, GRID_H, GRID_W])
                    steps.link(nc.gpsimd.tensor_tensor(grid(cacc), grid(cacc), rec, ALU.mult))
                    c = SEQ
                    if l < DEPTH - 1:
                        steps.link(nc.gpsimd.tensor_copy(cacc[:, SEQ:NT], src[:, SEQ:NT]))
                        for o in shifts:
                            a, b = SEQ + max(0, -o), NT - max(0, o)
                            steps.link(nc.gpsimd.tensor_tensor(cacc[:, a:b], cacc[:, a:b], src[:, a + o:b + o], ALU.add))
                        steps.link(nc.gpsimd.tensor_tensor(cacc[:, SEQ:NT], cacc[:, SEQ:NT],
                                                           recs[:, g, GRID_H:GRID_H + CTX], ALU.mult))
                        c = NT
                    nc.gpsimd.tensor_tensor(src[:, 0:c], cacc[:, 0:c], src[:, 0:c], ALU.subtract).then_inc(pooled, 1)
                    pool.wait_ge(pooled, 4 * l + g + 1)

            def clear_squares(n):
                if n:
                    pool.wait_ge(var_ready, n)
                steps.link(nc.gpsimd.memset(ssq[:], 0.0))

            clear_squares(0)
            for j in range(DC):
                add_squares(0, j, j % 2, BOTH)
            for ph in plan:
                l, kind, u0, p0 = ph["layer"], ph["kind"], ph["unit"], ph["pair"]
                if kind == "proj":
                    pool_groups(l, p0)
                    pool.wait_ge(w_used, u0 + ph["units"])
                    pool.wait_ge(misc_ready, MISC * (l + 1))
                    nc.gpsimd.memset(qbd[:], 0.0)
                    nc.gpsimd.memset(kpad[:], 0.0)
                    nc.gpsimd.memset(att[:], 0.0).then_inc(gla_zero, 1)
                elif last_norm_out(ph):
                    n = norm_of[(l, kind, ph["ffn"])]
                    pool.wait_ge(w_used, u0 + 2)
                    clear_squares(n)

                    def body(i):
                        for s in range(4):
                            add_squares(n, 4 * i + s, s % 2, phase_parts(ph))
                    repeat(pool, 0, 2, False, body)



_INS = ["x", "c", "ctx", "c_ctx", "w_mod", "b_mod", "norm_w", "ffn1_up", "ffn1_down", "w_in", "w_af_up", "b_af",
        "w_ab_up", "b_ab", "gla_norm_w", "pool_w", "pool_scale", "w_br_pool", "w_br_gla", "w_out",
        "ffn2_up", "ffn2_down", "final_norm_w"]


def constants():
    source, target = np.arange(P)[:, None], np.arange(P)[None, :]
    same = source // CHUNK == target // CHUNK
    forward, backward = same & (source <= target), same & (source > target)
    mask = np.concatenate([forward, forward, backward, backward], axis=1).astype(np.float32)
    recs = []
    for w in WINDOWS:
        sizes = [np.clip(np.arange(n) + w // 2, 0, n) - np.clip(np.arange(n) - w // 2, 0, n) for n in (GRID_H, CTX)]
        recs.append(1.0 / np.concatenate(sizes))
    return {
        "const_ident": np.eye(P, dtype=np.float32),
        "const_mask": mask,
        "const_reset": (np.arange(NT) % CHUNK != 0).astype(np.float32),
        "const_pool": np.array(recs, np.float32),
    }


def kernel(**inputs):
    import concourse.bacc as _bacc
    from concourse.bass_utils import run_bass_kernel_spmd as _run

    nc = _bacc.Bacc("TRN2", target_bir_lowering=False, num_devices=1)
    arrays, t = {}, {}
    named = {n: np.ascontiguousarray(inputs[n]) for n in _INS}
    named.update(constants())
    for name, a in named.items():
        arrays[f"in_{name}"] = a
        t[name] = nc.dram_tensor(f"in_{name}", a.shape, mybir.dt.from_np(a.dtype), kind="ExternalInput").ap()
    t["out"] = nc.dram_tensor("out_dram", (1, SEQ, D), F32, kind="ExternalOutput").ap()
    build(nc, t)
    r = _run(nc, [arrays], core_ids=[0])
    return r.results[0]["out_dram"]
```

```python
from contextlib import ExitStack

import numpy as np

import concourse.bass as bass
from concourse import mybir

P = 128
D = 1024
SEQ = 512
CTX = 256
NT = SEQ + CTX
DEPTH = 2
GRID_W = 64
GRID_H = SEQ // GRID_W
WINDOWS = (2, 4, 8, 16)
HEADS = 4
DK = 64
DV = 128
KW = HEADS * DK
VW = HEADS * DV
RANK = 16
TAU = 16.0
CHUNK = 64
D_FF = 2816
N_MOD = 9
EPS = 1e-6
POOLW = 512
OFF_K = 0
OFF_V = OFF_K + KW
OFF_AF = OFF_V + VW
OFF_Q = OFF_AF + 2 * RANK
OFF_R = OFF_Q + KW
OFF_POOL = OFF_R + VW
OFF_GP = OFF_POOL + POOLW
OFF_GG = OFF_GP + D

DC = D // P
NCH = NT // CHUNK
NBLK = NT // P
XBLK = SEQ // P
MODC = N_MOD * DC
MODJ = MODC // 2
START_JOBS = 2 * DC // 2
THIRDS = ((0, 8), (8, 8), (16, 6))
SQ_ADDED = DC - 2
FIRST_BANKS = (4, 0, 1, 2)
POOL_REC = GRID_H + GRID_W
POOL_PAD = GRID_H * (GRID_W + 8)

F32 = mybir.dt.float32
F32R = mybir.dt.float32r
U8 = mybir.dt.uint8
ALU = mybir.AluOpType
ACT = mybir.ActivationFunctionType
ds = bass.ds

ROW_BMOD, ROW_NORM = 0, MODC
ROW_BAF = ROW_NORM + 3 * DC
ROW_BAB = ROW_BAF + 2
ROW_GN = ROW_BAB + 2
ROW_PS = ROW_GN + 1
ROW_X1 = ROW_PS + 4
ROW_X2 = ROW_X1 + DC
ROWS = (ROW_X2 + DC, ROW_X2)

BOTH = ((0, SEQ), (SEQ, CTX))
LATENT = ((0, SEQ),)


def make_plan():
    plan, unit, pair, job = [], 0, 0, START_JOBS

    def add(kind, layer, pairs, ffn=0, third=0, jobs=0, units=None):
        nonlocal unit, pair, job
        units = 2 * pairs if units is None else units
        plan.append(dict(kind=kind, layer=layer, ffn=ffn, third=third, unit=unit, pair=pair,
                         pairs=pairs, units=units, job=job if plan else job - 2, jobs=jobs))
        unit, pair, job = unit + units, pair + pairs, job + jobs

    def add_ffn(layer, ffn, jobs):
        for t, (_, n) in enumerate(THIRDS):
            add("up", layer, n, ffn, t, jobs[2 * t])
            add("down", layer, DC // 2, ffn, t, jobs[2 * t + 1])

    left = DEPTH * MODJ - START_JOBS
    slots = [n for _, k in THIRDS for n in (k, DC // 2)]
    for layer in range(DEPTH):
        for ffn in range(2):
            first = layer == 0 and ffn == 0
            if ffn == 1:
                add("proj", layer, 9, units=17)
                add("gates", layer, 2 * DC)
                add("out", layer, DC // 2)
            jobs = []
            for s, n in enumerate(slots):
                room = n if not first else (n - 2, 4, 8, 4, 6, 4)[s]
                take = min(room, left)
                jobs.append(take)
                left -= take
            add_ffn(layer, ffn, jobs)
    assert left == 0
    return plan


def proj_pairs():
    two = lambda what, off, i: [(what, off + (2 * i + s) * P, P, 2 * i + s) for s in range(2)]
    return [two("k", OFF_K, 0), [("a", OFF_AF, 2 * RANK, 0)], two("q", OFF_Q, 0),
            two("u", OFF_POOL, 0), two("u", OFF_POOL, 1), two("v", OFF_V, 0), two("v", OFF_V, 1),
            two("r", OFF_R, 0), two("r", OFF_R, 1)]


PROJ_JOBS = {2: [("z", 0)], 3: [("z", 1)], 4: [("z", 2)], 5: [("z", 3)],
             6: [("vt", 0), ("vt", 1)], 7: [("vt", 2), ("vt", 3)] + [("pw", g) for g in range(4)]}
MISC = 12
FWD = [*range(SEQ // CHUNK, NCH), *range(SEQ // CHUNK)]
BWD = [*range(NCH - 1, SEQ // CHUNK - 1, -1), *range(SEQ // CHUNK - 1, -1, -1)]


def parts_of(kind, layer, what=None):
    if layer == DEPTH - 1 and (kind in ("gates", "out") or what in ("q", "r", "u")):
        return LATENT
    return BOTH


def phase_parts(ph):
    if ph["layer"] == DEPTH - 1 and ph["ffn"] == 1 and ph["kind"] in ("up", "down"):
        return LATENT
    return parts_of(ph["kind"], ph["layer"])


def build(nc, t):
    plan = make_plan()
    ctx = ExitStack()

    def sem(name):
        return ctx.enter_context(nc.semaphore(name))

    def sb(name, shape, dt=F32):
        return ctx.enter_context(nc.sbuf_tensor(name, shape, dt))

    x = sb("x", [P, DC * NT])
    wraw = sb("wraw", [P, 4, DC, P])
    whi = sb("whi", [P, 2, DC, P], F32R)
    wlo = sb("wlo", [P, 2, DC, P], F32R)
    modv = sb("modv", [P, 2 * DEPTH * MODC])
    vecs = sb("vecs", [P, 2, P])
    ident = sb("ident", [P, P])
    ones = sb("ones", [P, P])
    masks = sb("masks", [P, 2, 2 * P], U8)
    gate = sb("gate", [P, 2 * DC])
    amul = sb("amul", [P, 2 * DC])
    cond = sb("cond", [P, 2 * DC])
    eps = sb("eps", [P, 1])
    rstd = sb("rstd", [P, NT])
    tok = sb("tok", [P, HEADS * NBLK])

    class Layout:

        def __init__(self):
            self.stack, self.n = ExitStack(), 0

        def __call__(self, name, shape, dt=F32):
            return self.stack.enter_context(nc.sbuf_tensor(name, shape, dt))

        def skip(self, kib, name):
            return self(name, [P, kib * 256])

        def done(self):
            self.stack.close()

    lay = Layout()
    hhi = lay("hhi", [P, DC * NT], F32R)
    hlo = lay("hlo", [P, DC * NT], F32R)
    mhi = lay("mhi", [P, DC * NT], F32R)
    mlo = lay("mlo", [P, DC * NT], F32R)
    yphi = lay("yphi", [P, 4 * NT], F32R)
    yplo = lay("yplo", [P, 4 * NT], F32R)
    yghi = lay("yghi", [P, 4 * NT], F32R)
    yglo = lay("yglo", [P, 4 * NT], F32R)
    lay.done()

    lay = Layout()
    first_mod = lay("first_mod", [P, START_JOBS - 2, DC, 2 * P])
    xrow = lay("xrow", [P, NBLK, D])
    vrow = lay("vrow", [P, 2, P])
    mrow = lay("mrow", [P, 4 * P])
    mod_row = lay("mod_row", [P, 2 * P * START_JOBS])
    lay.done()

    lay = Layout()
    lay.skip(96, "pad_ffn")
    ssq = lay("ssq", [P, NT])
    sq = lay("sq", [P, 2, NT])
    htmp = lay("htmp", [P, 2, NT])
    stmp = lay("stmp", [P, 2, NT])
    mtmp = lay("mtmp", [P, 2, NT])
    modraw = lay("modraw", [P, 2, DC, 2 * P])
    macc = lay("macc", [P, 2, 2, 2 * P])
    lay.done()

    lay = Layout()
    lay.skip(48, "pad_proj")
    kq = lay("kq", [P, 4, NT])
    vt = lay("vt", [P, NBLK, VW])
    rsil = lay("rsil", [P, 4, NT])
    bsum = lay("bsum", [P, 4, NT])
    vf = lay("vf", [P, 2, NT])
    z = lay("z", [P, 3, NT])
    reset = lay("reset", [P, NT])
    alow = lay("alow", [P, NT])
    wup = lay("wup", [P, 2, KW])
    lay.skip(1, "pad_proj2")
    u = lay("u", [P, 4, NT])
    racc = lay("racc", [P, SEQ])
    padded = [lay(f"padded{i}", [P, POOL_PAD]) for i in range(2)]
    poolw = lay("poolw", [P, 4, P])
    recs = lay("recs", [P, 4, POOL_REC])
    lay.done()

    lay = Layout()
    qbd = lay("qbd", [P, 2, 2, NT])
    kt = lay("kt", [P, 2, NT])
    kpad = lay("kpad", [P, 2, NBLK, 2, P])
    states = lay("states", [P, 2, NCH, DV])
    lay.skip(6, "pad_gla")
    lay.skip(48 + 24, "pad_gla2")
    ex = lay("ex", [P, 2, 3, NT])
    att = lay("att", [P, 2, 2 * P])
    dec = lay("dec", [P, 2, NCH])
    lay.done()

    lay = Layout()
    lay.skip(120, "pad_onorm")
    osq = lay("osq", [P, HEADS, NT])
    lay.done()

    lay = Layout()
    lay.skip(48, "pad_merge")
    mf = lay("mf", [P, 2, DC * NT])
    lay.done()

    lay = Layout()
    lay.skip(48, "pad_end")
    orow = lay("orow", [P, XBLK, D])
    lay.done()

    ps = ctx.enter_context(nc.psum_tensor("ps", [P, 8 * 512], F32))

    def bank(b, c0=0, n=512):
        return ps[:, 512 * b + c0:512 * b + c0 + n]

    def pair_ps(b, s, part, rows=P):
        t0, n = part
        c = 512 * (3 * b + s) if t0 == 0 else 512 * (3 * b + 2) + CTX * s
        return ps[0:rows, c:c + n]

    w_loaded = [sem(f"w_loaded{i}") for i in range(4)]
    hi_split = sem("hi_split")
    lo_split = sem("lo_split")
    w_used = sem("w_used")
    pair_free = sem("pair_free")
    silu_done = sem("silu_done")
    mhi_done = sem("mhi_done")
    m_ready = sem("m_ready")
    s_const = sem("s_const")
    s_x = [sem(f"x_landed{i}") for i in range(2)]
    s_rows = sem("s_rows")
    s_mix = sem("s_mix")
    set_up = sem("set_up")
    vec_t = sem("vec_t")
    vec_ready = sem("vec_ready")
    cond_ready = sem("cond_ready")
    xt_ready = sem("xt_ready")
    xt_used = sem("xt_used")
    mod_loaded = [sem(f"mod_loaded{i}") for i in range(2)]
    first_loaded = [sem(f"first_loaded{i}") for i in range(START_JOBS)]
    first_row = sem("first_row")
    first_t = sem("first_t")
    mod_step = sem("mod_step")
    mod_sum = sem("mod_sum")
    mod_done = sem("mod_done")
    sq_ready = sem("sq_ready")
    sq_used = sem("sq_used")
    var_ready = sem("var_ready")
    std_ready = sem("std_ready")
    rec_ready = sem("rec_ready")
    bc_ready = sem("bc_ready")
    ht_ready = sem("ht_ready")
    hhi_ready = sem("hhi_ready")
    h_ready = sem("h_ready")
    pooled = sem("pooled")
    misc_ready = sem("misc_ready")
    misc_free = sem("misc_free")
    z_abs = sem("z_abs")
    z_log = sem("z_log")
    yp_hi = sem("yp_hi")
    b_ready = sem("b_ready")
    gla_zero = sem("gla_zero")
    d_ready = sem("d_ready")
    eend_ready = sem("eend_ready")
    e_ready = sem("e_ready")
    prep_ready = sem("prep_ready")
    kend_ready = sem("kend_ready")
    kend_t = sem("kend_t")
    kpad_ready = sem("kpad_ready")
    kv_ready = sem("kv_ready")
    kv_used = sem("kv_used")
    s_ready = sem("s_ready")
    att_ready = sem("att_ready")
    o_ready = sem("o_ready")
    o_used = sem("o_used")
    osq_ready = sem("osq_ready")
    ovar_ready = sem("ovar_ready")
    ostd_ready = sem("ostd_ready")
    orec_ready = sem("orec_ready")
    obc_ready = sem("obc_ready")
    oscaled = sem("oscaled")
    oy_ready = sem("oy_ready")
    yghi_ready = sem("yghi_ready")
    yg_ready = sem("yg_ready")
    merge_ready = sem("merge_ready")
    out_t = sem("out_t")
    out_row = sem("out_row")
    stored = sem("stored")
    pool_step = sem("pool_step")
    dve_step = sem("dve_step")
    act_step = sem("act_step")

    def repeat(eng, start, end, first, body):
        if first and start < end:
            body(start)
            start += 1
        if end - start == 1:
            body(start)
        elif end > start:
            with eng.Fori(start, end) as i:
                body(i)

    def segments(ph):
        if ph is plan[-1]:
            return [(a, a + 1, False) for a in range(ph["pairs"] // 2)]
        j0 = 1 if ph is plan[0] else 0
        j = j0 + ph["jobs"] // 2
        return [(a, b, w) for a, b, w in ((0, j0, False), (j0, j, True), (j, ph["pairs"] // 2, False)) if a < b]

    def at_least(eng, s, value):
        if not isinstance(value, int) or value > 0:
            eng.wait_ge(s, value)

    def first_mod_columns(j):
        n = START_JOBS - 2
        return first_mod[:, j] if j < n else modraw[:, j - n]

    def first_mod_ps(j):
        b = FIRST_BANKS[j // 2]
        return ps[0:2, 512 * b + 2 * P * (j % 2):512 * b + 2 * P * (j % 2 + 1)]

    class Steps:

        def __init__(self, eng, s):
            self.eng, self.s, self.n = eng, s, 0

        def link(self, ins):
            self.n += 1
            ins.then_inc(self.s, 1)
            self.eng.wait_ge(self.s, self.n)

    def last_norm_out(ph):
        return (ph["kind"] == "down" and ph["third"] == 2) or ph["kind"] == "out"

    norm_of = {}
    for n_, ph_ in enumerate([p for p in plan if last_norm_out(p)]):
        norm_of[(ph_["layer"], ph_["kind"], ph_["ffn"])] = n_ + 1

    def m_base(l, ffn, third=0):
        hidden = sum(n for _, n in THIRDS)
        return hidden * (2 * l + ffn) + DC * (l + ffn) + sum(n for _, n in THIRDS[:third])

    def m_base_merge(l):
        return m_base(l, 1) - DC

    def h_base(a):
        return 2 * DC * a - DC * max(0, a - (4 * DEPTH - 2))

    def follows_norm(ph):
        return ph["kind"] in ("proj", "gates") or (ph["kind"] == "up" and ph["third"] == 0)

    def second_unit(ph):
        unit = ph["unit"] + 1
        return unit, unit % 4, unit % 2

    def is_split_ahead(ph, i, h, s):
        return follows_norm(ph) and isinstance(i, int) and i == h == 0 and s == 1

    def peeled(ph, a):
        return (a == 0 and follows_norm(ph)) or (a == 1 and ph is plan[0])

    def proj_tensor(pe, l, u0, p0, unit_products, first_pair):
        unit, misc = u0, MISC * l
        for n, units in enumerate(proj_pairs()):
            pair = p0 + n
            pe.wait_ge(pair_free, pair - 1)
            if n == 0:
                first_pair(unit, pair % 2, BOTH, h_base(4 * l + 1))
                unit += 2
                continue
            for s, (what, _, _, _) in enumerate(units):
                outs = [(pt, pair_ps(pair % 2, s, pt)) for pt in parts_of("proj", l, what)]
                mm = unit_products(unit, unit % 2, DC, hhi, hlo, outs, None)
                mm.then_inc(w_used, 1)
                unit += 1
            for job, g in PROJ_JOBS.get(n, []):
                at_least(pe, misc_free, misc)
                if job == "z":
                    pr, d = g // 2, g % 2
                    pe.wait_ge(pair_free, p0 + 2)
                    pe.wait_ge(s_mix, 16 * 5 * (l + 1))
                    for t0, c in BOTH:
                        mm = nc.tensor.matmul(ps[:, 3072 + t0:3072 + t0 + c],
                                              wup[0:2 * RANK, d, pr * P:(pr + 1) * P],
                                              alow[0:2 * RANK, t0:t0 + c], start=True, stop=True)
                elif job == "vt":
                    pe.wait_ge(pair_free, p0 + (6, 7)[g // 2])
                    for b in range(NBLK):
                        mm = nc.tensor.transpose(bank(6, b * P, P), vf[:, g % 2, b * P:(b + 1) * P], ident[:])
                else:
                    pe.wait_ge(pooled, 4 * l + g + 1)
                    for t0, c in parts_of("proj", l, "u"):
                        mm = nc.tensor.matmul(ps[:, 3072 + t0:3072 + t0 + c], poolw[:, g, :],
                                              u[:, g, t0:t0 + c], start=True, stop=True)
                mm.then_inc(misc_ready, 1)
                misc += 1

    def blocks(l):
        return NBLK if l < DEPTH - 1 else XBLK

    def o_before(l, pr):
        return 2 * sum(blocks(i) for i in range(l)) + pr * blocks(l)

    KV_STEPS = NCH - 1

    def gla_tensor(pe, l, p0):
        pe.wait_ge(pair_free, p0 + 9)
        pe.wait_ge(misc_free, MISC * (l + 1))

        def transpose_kend(pr, d):
            pe.wait_ge(kend_ready, 4 * l + 2 * pr + d + 1)
            if pr and d:
                pe.wait_ge(kpad_ready, 4 * l + 3)
            for b in range(NBLK):
                mm = nc.tensor.transpose(kend_bank(pr, d, b * P, P), ex[:, d, 2, b * P:(b + 1) * P], ident[:])
            mm.then_inc(kend_t, 1)

        for d in range(2):
            transpose_kend(0, d)
        for pr in range(2):
            ob, nb, kv0 = o_before(l, pr), blocks(l), (2 * l + pr) * KV_STEPS

            def scores(b):
                at_least(pe, att_ready, ob + b - 1)
                for d in range(2):
                    mm = nc.tensor.matmul(bank(6 + b % 2, d * 2 * P, 2 * P), kt[:, d, b * P:(b + 1) * P],
                                          qbd[:, d, :, b * P:(b + 1) * P], start=True, stop=True)
                mm.then_inc(s_ready, 1)

            def kv_products(s):
                at_least(pe, kv_used, kv0 + s - 1)
                for d, order in enumerate((FWD, BWD)):
                    c = order[s]
                    mm = nc.tensor.matmul(bank(4 + s % 2, d * 2 * P, 2 * P), kpad[:, d, c // 2, c % 2, :],
                                          vt[:, c // 2, 2 * pr * DV:2 * (pr + 1) * DV], start=True, stop=True)
                mm.then_inc(kv_ready, 1)

            pe.wait_ge(kpad_ready, 4 * l + 2 * pr + 2)
            kv_products(0)
            kv_products(1)
            pe.wait_ge(prep_ready, 4 * l + 2 * pr + 2)
            pe.wait_ge(gla_zero, 2 * (l + 1))
            scores(0)
            scores(1)
            for s in range(2, KV_STEPS):
                kv_products(s)
            pe.wait_ge(kv_used, kv0 + KV_STEPS)
            for b in range(nb):
                pe.wait_ge(att_ready, ob + b + 1)
                at_least(pe, o_used, ob + b - 1)
                o = bank(b % 2, 0, 2 * P)
                terms = [(o[:, h * P:(h + 1) * P], vt[:, b, (2 * pr + h) * DV:(2 * pr + h + 1) * DV],
                          att[:, b % 2, h * P:(h + 1) * P]) for h in range(2)]
                for half in range(2):
                    c = 2 * b + half
                    for d, order in enumerate((FWD, BWD)):
                        if c != order[0]:
                            terms.append((o.rearrange("p (h c) -> p h c", h=2)[:, :, half * CHUNK:(half + 1) * CHUNK],
                                          states[:, d, c, :],
                                          qbd[:, d, :, c * CHUNK:(c + 1) * CHUNK]))
                for n, (out, lhsT, rhs) in enumerate(terms):
                    mm = nc.tensor.matmul(out, lhsT, rhs, start=(n == 0), stop=(n == len(terms) - 1),
                                          skip_group_check=True)
                mm.then_inc(o_ready, 1)
                if b + 2 < nb:
                    scores(b + 2)
                if pr == 0 and b in (1, 2):
                    transpose_kend(1, b - 1)
        for h in range(HEADS):
            pe.wait_ge(osq_ready, 4 * l + h + 1)
            for b in range(nb):
                mm = nc.tensor.matmul(bank(7, h * NBLK + b, 1), osq[:, h, b * P:(b + 1) * P], ones[:, 0:1],
                                      start=True, stop=True)
        mm.then_inc(ovar_ready, 1)

    def kend_bank(pr, d, c0, n):
        return bank(2 * d if pr == 0 else 2, c0, n)

    def onorm_ps(h, buf):
        c = 3072 if h in (0, 3) else 1536 * (1 - buf) + NT * (h - 1)
        return ps[:, c:c + NT]

    def onorm_tensor(pe, l, buf, heads):
        pe.wait_ge(orec_ready, l + 1)
        for h in heads:
            if h == 3:
                pe.wait_ge(oy_ready, 4 * l + 1)
            for b in range(blocks(l)):
                mm = nc.tensor.transpose(onorm_ps(h, buf)[:, b * P:(b + 1) * P],
                                         tok[:, h * NBLK + b:h * NBLK + b + 1].to_broadcast([P, P]), ident[:])
            mm.then_inc(obc_ready, 1)

    def w_load_count(unit, slot4):
        return 4 * unit + (16 - 4 * slot4)

    def proj_scalar(act, steps, l, u0, p0, split_hi):
        unit, misc = u0, MISC * l
        for n, units in enumerate(proj_pairs()):
            for s in range(1 if n else 2, len(units) + 1):
                split_hi(unit + s, (unit + s) % 4, (unit + s) % 2)
            unit += len(units)
            buf, what = (p0 + n) % 2, units[0][0]
            parts = parts_of("proj", l, what)
            if what in "akur":
                act.wait_ge(w_used, unit)
                act.wait_ge(pair_free, p0 + n)
                for s, (_, _, m, idx) in enumerate(units):
                    for pt in parts:
                        t0, c = pt
                        dst = {"a": alow[0:m, t0:t0 + c], "k": kq[:, idx % 4, t0:t0 + c], "u": u[:, idx % 4, t0:t0 + c],
                               "r": rsil[:, idx % 4, t0:t0 + c]}[what]
                        ins = nc.scalar.activation(dst, pair_ps(buf, s, pt, m), ACT.Silu if what == "r" else ACT.Copy)
                ins.then_inc(pair_free, 1)
            for job, g in PROJ_JOBS.get(n, []):
                misc += 1
                if job == "z":
                    pr, d = g // 2, g % 2
                    row = (ROW_BAF, ROW_BAB)[d] + pr
                    act.wait_ge(misc_ready, misc)
                    at_least(act, b_ready, 4 * l + g)
                    nc.scalar.activation(z[:, 0, :], ps[:, 3072:3072 + NT], ACT.Abs,
                                         bias=vecs[:, l, row:row + 1]).then_inc(z_abs, 1)
                    act.wait_ge(z_abs, 4 * l + g + 1)
                    steps.link(nc.scalar.activation(z[:, 0, :], z[:, 0, :], ACT.Exp, scale=-1.0))
                    nc.scalar.activation(z[:, 0, :], z[:, 0, :], ACT.Ln, bias=1.0).then_inc(z_log, 1)
                elif job == "pw":
                    act.wait_ge(misc_ready, misc)
                    act.wait_ge(misc_free, MISC * l + 8)
                    c = sum(pt[1] for pt in parts_of("proj", l, "u"))
                    nc.scalar.activation(yphi[:, g * NT:g * NT + c], ps[:, 3072:3072 + c], ACT.Copy,
                                         scale=vecs[:, l, ROW_PS + g:ROW_PS + g + 1]).then_inc(yp_hi, 1)

    def gla_scalar(act, steps, l, hi_chunk, split_gates):
        nb = blocks(l)
        c = nb * P

        def exponentials(pr):
            if pr:
                act.wait_ge(prep_ready, 4 * l + 2)
            for d in range(2):
                b = bsum[:, 2 * pr + d, :]
                end = b.rearrange("p (n c) -> p n c", c=CHUNK)[:, :, (CHUNK - 1, 0)[d]]
                act.wait_ge(d_ready, 4 * l + 2 * pr + d + 1)
                nc.scalar.activation(ex[:, d, 2, :], ex[:, d, 2, :], ACT.Exp, scale=1.0 / TAU).then_inc(eend_ready, 1)
            for d in range(2):
                b = bsum[:, 2 * pr + d, :]
                end = b.rearrange("p (n c) -> p n c", c=CHUNK)[:, :, (CHUNK - 1, 0)[d]]
                nc.scalar.activation(ex[:, d, 1, :], b, ACT.Exp, scale=-1.0 / TAU)
                nc.scalar.activation(ex[:, d, 0, :], b, ACT.Exp, scale=1.0 / TAU)
                if pr and d == 0:
                    act.wait_ge(kv_used, (2 * l + 1) * KV_STEPS)
                nc.scalar.activation(dec[:, d, :], end, ACT.Exp, scale=1.0 / TAU).then_inc(e_ready, 1)

        def pad_kend(pr, d):
            act.wait_ge(kend_t, 4 * l + 2 * pr + d + 1)
            src = kend_bank(pr, d, 0, NT).rearrange("p (b n) -> p b n", b=NBLK)
            nc.scalar.activation(kpad[0:CHUNK, d, :, 0, :], src[0:CHUNK], ACT.Copy)
            nc.scalar.activation(kpad[CHUNK:P, d, :, 1, :], src[CHUNK:P], ACT.Copy).then_inc(kpad_ready, 1)

        def square_outputs(pr):
            act.wait_ge(o_used, o_before(l, pr) + nb)
            for h in (2 * pr, 2 * pr + 1):
                nc.scalar.activation(osq[:, h, 0:c], bsum[:, h, 0:c], ACT.Square).then_inc(osq_ready, 1)

        exponentials(0)
        act.wait_ge(gla_zero, 2 * l + 1)
        for d in range(2):
            pad_kend(0, d)
        exponentials(1)
        for pr in range(2):
            ob = o_before(l, pr)
            if pr:
                act.wait_ge(prep_ready, 4 * l + 4)
                act.wait_ge(kend_t, 4 * l + 4)
                square_outputs(0)
            for b in range(nb):
                act.wait_ge(o_ready, ob + b + 1)
                nc.scalar.activation(bsum[:, 2 * pr:2 * pr + 2, b * P:(b + 1) * P],
                                     bank(b % 2, 0, 2 * P).rearrange("p (h n) -> p h n", h=2),
                                     ACT.Copy).then_inc(o_used, 1)
                if pr == 0 and b in (1, 2):
                    pad_kend(1, b - 1)
        square_outputs(1)
        split_gates()
        for i in range(DC * len(parts_of("gates", l))):
            hi_chunk(i)
            if i == 4:
                act.wait_ge(ovar_ready, l + 1)
                src = bank(7, 0, HEADS * NBLK).rearrange("p (h b) -> p h b", h=HEADS)[:, :, 0:nb]
                nc.scalar.activation(tok[:].rearrange("p (h b) -> p h b", h=HEADS)[:, :, 0:nb], src, ACT.Sqrt,
                                     bias=eps[:, 0:1], scale=1.0 / DV).then_inc(ostd_ready, 1)
        for h in range(HEADS):
            act.wait_ge(oy_ready, 4 * l + h + 1)
            nc.scalar.activation(yghi[:, h * NT:h * NT + c], bsum[:, h, 0:c], ACT.Copy).then_inc(yghi_ready, 1)

    def mod_needed(l, blocks_of_d):
        return l * MODJ + blocks_of_d * DC // 2

    def proj_vector(dve, steps, l, u0, p0, split_lo):
        nc.vector.memset(wup[:], 0.0).then_inc(set_up, 1)
        unit, misc = u0, MISC * l
        for n, units in enumerate(proj_pairs()):
            for s in range(1 if n else 2, len(units) + 1):
                split_lo(unit + s, (unit + s) % 4, (unit + s) % 2)
            unit += len(units)
            buf, what = (p0 + n) % 2, units[0][0]

            def read_out():
                dve.wait_ge(w_used, unit)
                dve.wait_ge(pair_free, p0 + n)
                if what == "v":
                    at_least(dve, misc_ready, MISC * l + 4 + units[0][3])
                for s, (_, _, m, idx) in enumerate(units):
                    for pt in parts_of("proj", l, what):
                        t0, c = pt
                        dst = kq[:, 2 + idx % 2, t0:t0 + c] if what == "q" else vf[:, s, t0:t0 + c]
                        ins = nc.vector.tensor_scalar(dst, pair_ps(buf, s, pt), DK ** -0.5 if what == "q" else 1.0,
                                                      None, ALU.mult)
                ins.then_inc(pair_free, 1)

            if what == "q" or (what == "v" and n not in PROJ_JOBS):
                read_out()
            for job, g in PROJ_JOBS.get(n, []):
                misc += 1
                if job == "z":
                    pr, d = g // 2, g % 2
                    row = (ROW_BAF, ROW_BAB)[d] + pr
                    dve.wait_ge(z_abs, 4 * l + g + 1)
                    nc.vector.tensor_scalar(z[:, 1, :], ps[:, 3072:3072 + NT], vecs[:, l, row:row + 1], 0.0,
                                            ALU.add, ALU.min).then_inc(misc_free, 1)
                    dve.wait_ge(z_log, 4 * l + g + 1)
                    dve.wait_ge(misc_free, misc)
                    steps.link(nc.vector.tensor_tensor(z[:, 1, :], z[:, 1, :], z[:, 0, :], ALU.subtract))
                    if g == 0:
                        dve.wait_ge(s_mix, 16 * 5 * (l + 1))
                    if d == 0:
                        nc.vector.tensor_tensor_scan(bsum[:, g, :], reset[:], z[:, 1, :], 0.0, ALU.mult,
                                                     ALU.add).then_inc(b_ready, 1)
                    else:
                        steps.link(nc.vector.tensor_tensor_scan(z[:, 2, :], reset[:], z[:, 1, :], 0.0, ALU.mult, ALU.add))
                        zc = z[:, 2, :].rearrange("p (n c) -> p n c", c=CHUNK)
                        steps.link(nc.vector.tensor_tensor(
                            z[:, 0, :].rearrange("p (n c) -> p n c", c=CHUNK),
                            zc[:, :, CHUNK - 1:CHUNK].to_broadcast([P, NCH, CHUNK]), zc, ALU.subtract))
                        nc.vector.tensor_tensor(bsum[:, g, :], z[:, 0, :], z[:, 1, :], ALU.add).then_inc(b_ready, 1)
                elif job == "vt":
                    dve.wait_ge(misc_ready, misc)
                    nc.vector.tensor_copy(vt[:, :, g * DV:(g + 1) * DV],
                                          bank(6, 0, NT).rearrange("p (b n) -> p b n", b=NBLK)).then_inc(misc_free, 1)
                else:
                    c = sum(pt[1] for pt in parts_of("proj", l, "u"))
                    dve.wait_ge(yp_hi, 4 * l + g + 1)
                    nc.vector.scalar_tensor_tensor(
                        out=yplo[:, g * NT:g * NT + c], in0=ps[:, 3072:3072 + c],
                        scalar=vecs[:, l, ROW_PS + g:ROW_PS + g + 1], in1=yphi[:, g * NT:g * NT + c].bitcast(F32),
                        op0=ALU.mult, op1=ALU.subtract).then_inc(misc_free, 1)
            if what == "v" and n in PROJ_JOBS:
                read_out()

    def gla_vector(dve, steps, l, u0, h_steps, split_gates):
        nb = blocks(l)
        c = nb * P

        def to_end(pr):
            at_least(dve, kend_t, 4 * l + 2 * pr)
            for d in range(2):
                b = bsum[:, 2 * pr + d, :].rearrange("p (n c) -> p n c", c=CHUNK)
                e = (CHUNK - 1, 0)[d]
                nc.vector.tensor_tensor(ex[:, d, 2, :].rearrange("p (n c) -> p n c", c=CHUNK),
                                        b[:, :, e:e + 1].to_broadcast([P, NCH, CHUNK]), b,
                                        ALU.subtract).then_inc(d_ready, 1)

        def scale_kend(pr):
            for d in range(2):
                dve.wait_ge(eend_ready, 4 * l + 2 * pr + d + 1)
                nc.vector.tensor_tensor(ex[:, d, 2, :], kq[:, pr, :], ex[:, d, 2, :], ALU.mult).then_inc(kend_ready, 1)

        def scale_qk(pr):
            for d in range(2):
                dve.wait_ge(e_ready, 4 * l + 2 * pr + d + 1)
                nc.vector.tensor_tensor(kt[:, d, :], kq[:, pr, :], ex[:, d, 1, :], ALU.mult)
                for h in range(2):
                    r = slice(h * DK, (h + 1) * DK)
                    ins = nc.vector.tensor_tensor(qbd[r, d, h, 0:c], kq[r, 2 + pr, 0:c], ex[r, d, 0, 0:c], ALU.mult)
                ins.then_inc(prep_ready, 1)

        dve.wait_ge(misc_ready, MISC * (l + 1))
        to_end(0)
        scale_kend(0)
        dve.wait_ge(w_used, u0 + 17)
        scale_qk(0)
        dve.wait_ge(gla_zero, 2 * (l + 1))
        for pr in range(2):
            ob, kv0 = o_before(l, pr), (2 * l + pr) * KV_STEPS

            def mask_scores(b):
                dve.wait_ge(s_ready, ob + b + 1)
                at_least(dve, o_ready, ob + b - 1)
                steps.link(nc.vector.copy_predicated(att[:, b % 2, :], masks[:, 0, :], bank(6 + b % 2, 0, 2 * P)))
                nc.vector.copy_predicated(att[:, b % 2, :], masks[:, 1, :],
                                          bank(6 + b % 2, 2 * P, 2 * P)).then_inc(att_ready, 1)

            mask_scores(0)
            mask_scores(1)
            if pr == 0:
                to_end(1)
            for s in range(KV_STEPS):
                dve.wait_ge(kv_ready, kv0 + s + 1)
                if s:
                    dve.wait_ge(kv_used, kv0 + s)
                for d, order in enumerate((FWD, BWD)):
                    ch, nxt = order[s], order[s + 1]
                    for h in range(2):
                        r = slice(h * DK, (h + 1) * DK)
                        kv = ps[r, 512 * (4 + s % 2) + d * 2 * P + h * DV:512 * (4 + s % 2) + d * 2 * P + (h + 1) * DV]
                        if s == 0:
                            ins = nc.vector.tensor_copy(states[r, d, nxt, :], kv)
                        else:
                            ins = nc.vector.scalar_tensor_tensor(
                                out=states[r, d, nxt, :], in0=states[r, d, ch, :], scalar=dec[r, d, ch:ch + 1],
                                in1=kv, op0=ALU.mult, op1=ALU.add)
                ins.then_inc(kv_used, 1)
            for b in range(2, nb):
                mask_scores(b)
                if pr == 0 and b == 2:
                    scale_kend(1)
            dve.wait_ge(o_ready, ob + nb)
            if pr == 0:
                scale_qk(1)

        split_gates()
        for i, step in enumerate(h_steps):
            step()
            if i == 6:
                dve.wait_ge(ostd_ready, l + 1)
                v = tok[:].rearrange("p (h b) -> p h b", h=HEADS)[:, :, 0:nb]
                nc.vector.reciprocal(v, v).then_inc(orec_ready, 1)
        buf = gates_phase(l)["pair"] % 2
        for h in range(HEADS):
            dve.wait_ge(obc_ready, 4 * l + (1, 3, 3, 4)[h])
            dve.wait_ge(oscaled, 4 * l + h + 1)
            nc.vector.scalar_tensor_tensor(
                out=bsum[:, h, 0:c], in0=onorm_ps(h, buf)[:, 0:c], scalar=vecs[:, l, ROW_GN:ROW_GN + 1],
                in1=rsil[:, h, 0:c], op0=ALU.mult, op1=ALU.mult).then_inc(oy_ready, 1)
            if h:
                split_output(dve, l, h - 1, c)
        split_output(dve, l, HEADS - 1, c)

    def split_output(dve, l, h, c):
        dve.wait_ge(yghi_ready, 4 * l + h + 1)
        nc.vector.tensor_tensor(yglo[:, h * NT:h * NT + c], bsum[:, h, 0:c],
                                yghi[:, h * NT:h * NT + c].bitcast(F32), ALU.subtract).then_inc(yg_ready, 1)

    def gates_phase(l):
        return [ph for ph in plan if ph["kind"] == "gates"][l]


    with ctx:
        block = ctx.enter_context(nc.Block())

        @block.sync
        def _(sp):
            wm = [t["w_mod"][l].rearrange("(c p) n -> p c n", p=P) for l in range(DEPTH)]

            def load_mod(job, layer, buf):
                if isinstance(job, int) and job < START_JOBS + 2:
                    sp.wait_ge(mod_done, START_JOBS)
                else:
                    sp.wait_ge(mod_step, DC * 2 * (job - START_JOBS - 1))
                sp.dma_start(modraw[:, buf], wm[layer][:, :, ds((job - layer * MODJ) * 2 * P, 2 * P)]
                             ).then_inc(mod_loaded[buf], 16)

            def load_unit(unit, slot, src, k, cols=P):
                at_least(sp, lo_split, unit - 3)
                sp.dma_start(wraw[:, slot, 0:k, 0:cols], src).then_inc(w_loaded[slot], 16)

            for l in range(DEPTH):
                for name, row in (("b_mod", ROW_BMOD), ("norm_w", ROW_NORM), ("b_af", ROW_BAF),
                                  ("b_ab", ROW_BAB), ("gla_norm_w", ROW_GN), ("pool_scale", ROW_PS)):
                    src = t[name][l]
                    src = src.rearrange("a (r q) -> (a r) q", q=P) if len(src.shape) == 2 else \
                        src.rearrange("(r q) -> r q", q=P)
                    sp.dma_start(vrow[row:row + src.shape[0], l, :], src).then_inc(s_rows, 16)
            sp.dma_start(vrow[ROW_X1:ROW_X1 + DC, 0, :], t["c"][0].rearrange("(r q) -> r q", q=P)).then_inc(s_rows, 16)
            sp.dma_start(vrow[ROW_X2:ROW_X2 + DC, 0, :], t["c_ctx"].rearrange("(r q) -> r q", q=P)).then_inc(s_rows, 16)
            sp.dma_start(vrow[ROW_X1:ROW_X1 + DC, 1, :], t["final_norm_w"].rearrange("(r q) -> r q", q=P)).then_inc(s_rows, 16)
            for j in range(START_JOBS):
                sp.dma_start(first_mod_columns(j), wm[0][:, :, j * 2 * P:(j + 1) * 2 * P]).then_inc(first_loaded[j], 16)

            for ph in plan:
                l, kind, u0, j0 = ph["layer"], ph["kind"], ph["unit"], ph["job"]
                f0, fk = THIRDS[ph["third"]]
                up = t["ffn1_up" if ph["ffn"] == 0 else "ffn2_up"][l].rearrange("(c p) n -> p c n", p=P)
                down = t["ffn1_down" if ph["ffn"] == 0 else "ffn2_down"][l].rearrange("(c p) n -> p c n", p=P)
                w_in = t["w_in"][l].rearrange("(c p) n -> p c n", p=P)
                w_pool = t["w_br_pool"][l].rearrange("(c p) n -> p c n", p=P)
                w_gla = t["w_br_gla"][l].rearrange("(c p) n -> p c n", p=P)
                w_out = t["w_out"][l].rearrange("(c p) n -> p c n", p=P)
                if kind == "proj":
                    unit = u0
                    todo = [w for pair in proj_pairs() for w in pair]
                    for _, col, m, _ in todo[:3]:
                        load_unit(unit, unit % 4, w_in[:, :, col:col + m], DC, m)
                        unit += 1
                    sp.wait_ge(h_ready, h_base(4 * l + 2))
                    sp.dma_start(reset[:], t["const_reset"].partition_broadcast(P)).then_inc(s_mix, 16)
                    sp.dma_start(poolw[:], t["pool_w"][l].rearrange("g p q -> p g q")).then_inc(s_mix, 16)
                    sp.dma_start(recs[:], t["const_pool"].partition_broadcast(P)).then_inc(s_mix, 16)
                    sp.wait_ge(set_up, 2 + l)
                    sp.dma_start(wup[0:RANK, 0, :], t["w_af_up"][l]).then_inc(s_mix, 16)
                    sp.dma_start(wup[RANK:2 * RANK, 1, :], t["w_ab_up"][l]).then_inc(s_mix, 16)
                    for _, col, m, _ in todo[3:]:
                        load_unit(unit, unit % 4, w_in[:, :, col:col + m], DC, m)
                        unit += 1
                    continue
                for a, b, jobs in segments(ph):
                    def body(i, jobs=jobs):
                        nxt = sp.snap((i + 1) * P) if kind == "gates" else 0
                        for h in range(2):
                            for s in range(2):
                                unit = u0 + 4 * i + 2 * h + s
                                slot = (u0 + 2 * h + s) % 4
                                if kind == "up":
                                    src, k = up[:, :, ds((f0 + 2 * i + h) * P + s * D_FF, P)], DC
                                elif kind == "down":
                                    src, k = down[:, f0:f0 + fk, ds((4 * i + 2 * h + s) * P, P)], fk
                                elif kind == "out":
                                    src, k = w_out[:, :, ds((4 * i + 2 * h + s) * P, P)], DC
                                elif h == 0:
                                    src, k = w_in[:, :, ds(OFF_GP + s * D - P + nxt, P)], DC
                                else:
                                    src, k = (w_pool, w_gla)[s][:, :, ds(nxt - P, P)], 4
                                load_unit(unit, slot, src, k)
                            if jobs:
                                load_mod(j0 + 2 * i + h, (j0 >= MODJ) * 1, (j0 + h) % 2)
                    repeat(sp, a, b, ph is plan[0] and a < 2, body)

            sp.wait_ge(out_row, DC)
            for b in range(XBLK):
                sp.dma_start(t["out"][0, b * P:(b + 1) * P, :], orow[:, b, :]).then_inc(stored, 16)
            sp.wait_ge(stored, 16 * XBLK)

        @block.tensor
        def _(pe):
            def unit_products(unit, slot, kk, hi, lo, outs, chunk_wait):
                pe.wait_ge(lo_split, unit + 1)
                for k in range(kk):
                    if chunk_wait is not None:
                        pe.wait_ge(chunk_wait[0], chunk_wait[1] + k)
                    for w, a in ((whi, hi), (whi, lo), (wlo, hi)):
                        for (t0, n), o in outs:
                            last = k == kk - 1 and w is wlo
                            mm = nc.tensor.matmul(o, w[:, slot, k, :], a[:, k * NT + t0:k * NT + t0 + n],
                                                  start=(k == 0 and w is whi and a is hi), stop=last)
                return mm

            def first_pair(unit, buf, parts, base, between=lambda n_pt: None):
                pe.wait_ge(lo_split, unit + 2)
                for n_pt, pt in enumerate(parts):
                    t0, n = pt
                    tail = DC if n_pt < len(parts) - 1 else DC - (2 if t0 == 0 else 4)
                    order = [(k, s) for k in range(tail) for s in range(2)]
                    order += [(k, s) for s in range(2) for k in range(tail, DC)]
                    for k, s in order:
                        pe.wait_ge(h_ready, base + n_pt * DC + k + 1)
                        for w, a in ((whi, hhi), (whi, hlo), (wlo, hhi)):
                            mm = nc.tensor.matmul(
                                pair_ps(buf, s, pt), w[:, (unit + s) % 2, k, :], a[:, k * NT + t0:k * NT + t0 + n],
                                start=(k == 0 and w is whi and a is hhi and (t0 == 0 or s == 0)),
                                stop=(k == DC - 1 and w is wlo and (t0 == 0 or s == 1)),
                                skip_group_check=True)
                        if n_pt == len(parts) - 1 and k == DC - 1:
                            mm.then_inc(w_used, 1)
                    between(n_pt)

            def norm_sum(n, parts):
                if n == 0:
                    pe.wait_ge(set_up, 1)
                nb = sum(pt[1] for pt in parts) // P
                pe.wait_ge(sq_used, SQ_ADDED * (n + 1))
                for j in range(SQ_ADDED - 1, DC):
                    if j >= SQ_ADDED:
                        pe.wait_ge(sq_ready, DC * n + j + 1)
                    for b in range(nb):
                        src = (ssq if j < SQ_ADDED else sq[:, j % 2])[:, b * P:(b + 1) * P]
                        mm = nc.tensor.matmul(bank(7, 256 + b, 1), src, ones[:, 0:1], start=(j < SQ_ADDED and b == 0),
                                              stop=(j == DC - 1 and b == nb - 1), skip_group_check=True)
                mm.then_inc(var_ready, 1)
                if n:
                    pe.wait_ge(mod_done, min([p["job"] + p["jobs"] for p in plan if last_norm_out(p)][n - 1],
                                             DEPTH * MODJ))
                pe.wait_ge(rec_ready, n + 1)
                for b in range(nb):
                    mm = nc.tensor.transpose(bank(6, b * P, P), tok[:, b:b + 1].to_broadcast([P, P]), ident[:])
                mm.then_inc(bc_ready, 1)

            def mod_sums(job, buf):
                pe.wait_ge(mod_step, DC * 2 * (job + 1 - START_JOBS))
                for c in range(2):
                    for h in range(2):
                        mm = nc.tensor.matmul(bank(6, 2 * c + h, 1), macc[:, buf, c, h * P:(h + 1) * P],
                                              ones[:, 0:1], start=True, stop=True)
                mm.then_inc(mod_sum, 1)

            pe.wait_ge(s_const, 32)
            pe.wait_ge(s_rows, 16 * 15)
            for l in range(DEPTH):
                mm = nc.tensor.transpose(bank(7, l * P, ROWS[l]), vrow[0:ROWS[l], l, :], ident[0:ROWS[l], 0:ROWS[l]])
            mm.then_inc(vec_t, 1)
            for q in s_x:
                pe.wait_ge(q, 16)
            for j in range(DC):
                at_least(pe, xt_used, j - 1)
                for b in range(NBLK):
                    mm = nc.tensor.transpose(bank(2 * (j % 2), b * P, P), xrow[:, b, j * P:(j + 1) * P], ident[:])
                mm.then_inc(xt_ready, 1)
            pe.wait_ge(set_up, 1)
            def transpose_first_mod(i):
                pe.wait_ge(first_row, i + 1)
                for b in range(4 * i, 4 * i + 4):
                    mm = nc.tensor.transpose(bank(5, 2 * b, 2), mod_row[0:2, b * P:(b + 1) * P], ident[0:2, 0:2])
                mm.then_inc(first_t, 1)

            pe.wait_ge(cond_ready, 1)
            both = cond[:].rearrange("p (c k) -> p k c", c=2)
            for j in range(START_JOBS):
                if j == START_JOBS // 2:
                    norm_sum(0, BOTH)
                pe.wait_ge(first_loaded[j], 16)
                if j == 2:
                    pe.wait_ge(xt_used, DC)
                for k in range(DC):
                    mm = nc.tensor.matmul(first_mod_ps(j), both[:, k, :], first_mod_columns(j)[:, k, :],
                                          start=(k == 0), stop=(k == DC - 1))
                mm.then_inc(mod_sum, 1)
                if j % 2 == 0 and j:
                    transpose_first_mod(j // 2 - 1)
            transpose_first_mod(START_JOBS // 2 - 1)
            pe.wait_ge(xt_used, DC)

            for n_ph, ph in enumerate(plan):
                l, kind, u0, p0, j0 = ph["layer"], ph["kind"], ph["unit"], ph["pair"], ph["job"]
                fk = THIRDS[ph["third"]][1]
                parts = phase_parts(ph)
                if kind == "proj":
                    proj_tensor(pe, l, u0, p0, unit_products, first_pair)
                    gla_tensor(pe, l, p0)
                    continue
                if kind in ("up", "down"):
                    m_before = m_base(l, ph["ffn"], ph["third"])
                for a, b, jobs in segments(ph):
                    def body(i, jobs=jobs):
                        for h in range(2):
                            pair, buf = p0 + 2 * i + h, (p0 + h) % 2
                            at_least(pe, pair_free, pair - 1)
                            if is_split_ahead(ph, i, h, 1):
                                def between(n_pt):
                                    if kind == "gates" and n_pt == 0:
                                        onorm_tensor(pe, l, buf, (0, 1, 2))
                                    if kind == "gates" and n_pt == len(parts) - 1:
                                        onorm_tensor(pe, l, buf, (3,))
                                first_pair(u0, buf, parts, h_base(4 * l + (2 if kind == "gates" else 3 * ph["ffn"])),
                                           between)
                            for s in range(2):
                                if is_split_ahead(ph, i, h, 1):
                                    continue
                                unit, slot = u0 + 4 * i + 2 * h + s, (u0 + s) % 2
                                outs = [(pt, pair_ps(buf, s, pt)) for pt in parts]
                                first = h == 0 and s == 0
                                if kind == "up":
                                    mm = unit_products(unit, slot, DC, hhi, hlo, outs, None)
                                elif kind == "down":
                                    wait = (m_ready, m_before + 1) if first else None
                                    mm = unit_products(unit, slot, fk, mhi, mlo, outs, wait)
                                elif kind == "out":
                                    wait = (m_ready, m_base_merge(l) + 1) if first else None
                                    mm = unit_products(unit, slot, DC, mhi, mlo, outs, wait)
                                elif h == 0:
                                    mm = unit_products(unit, slot, DC, hhi, hlo, outs, None)
                                else:
                                    if s == 1:
                                        pe.wait_ge(yg_ready, 4 * (l + 1))
                                    mm = unit_products(unit, slot, 4, (yphi, yghi)[s], (yplo, yglo)[s], outs, None)
                                mm.then_inc(w_used, 1)
                            if jobs:
                                mod_sums(j0 + 2 * i + h, (j0 + h) % 2)
                            if kind == "gates" and h == 0 and isinstance(i, int) and i == 0:
                                pe.wait_ge(oy_ready, 4 * l + 3)
                    repeat(pe, a, b, peeled(ph, a), body)
                if last_norm_out(ph):
                    n = norm_of[(l, kind, ph["ffn"])]
                    last = n == 3 * DEPTH
                    norm_sum(n, phase_parts(plan[n_ph + 1]) if not last else LATENT)

            for j in range(DC):
                pe.wait_ge(ht_ready, h_base(4 * DEPTH) + j + 1)
                at_least(pe, out_row, j - 1)
                for b in range(XBLK):
                    mm = nc.tensor.transpose(bank(j % 2, b * P, P), htmp[:, j % 2, b * P:(b + 1) * P], ident[:])
                mm.then_inc(out_t, 1)

        @block.scalar
        def _(act):
            steps = Steps(act, act_step)

            def split_hi(unit, slot4, slot2):
                act.wait_ge(w_loaded[slot4], w_load_count(unit, slot4))
                at_least(act, w_used, unit - 1)
                nc.scalar.activation(whi[:, slot2], wraw[:, slot4], ACT.Copy).then_inc(hi_split, 1)

            def squares(n, j, parts):
                at_least(act, sq_used, SQ_ADDED * n + j - 1)
                c = sum(pt[1] for pt in parts)
                nc.scalar.activation(sq[:, (j if isinstance(j, int) else 0) % 2, 0:c], x[:, ds(j * NT, c)],
                                     ACT.Square).then_inc(sq_ready, 1)

            def norm_apply(a, n, nxt, which, tmp):
                l, parts = nxt["layer"], phase_parts(nxt)
                split_hi(*second_unit(nxt))
                act.wait_ge(var_ready, n + 1)
                root(sum(pt[1] for pt in parts) // P)
                for i in range(DC * len(parts)):
                    hi_chunk(i, a, l, which, parts, tmp)

            def root(nb):
                nc.scalar.activation(tok[:, 0:nb], bank(7, 256, nb), ACT.Sqrt, bias=eps[:, 0:1],
                                     scale=1.0 / D).then_inc(std_ready, 1)

            def hi_chunk(i, a, l, which, parts, tmp):
                act.wait_ge(ht_ready, h_base(a) + i + 1)
                c, j = divmod(i, DC)
                t0, m = parts[c]
                sh = c * DEPTH * MODC + l * MODC + 3 * which * DC + j
                nc.scalar.activation(hhi[:, j * NT + t0:j * NT + t0 + m], tmp(i)[:, t0:t0 + m],
                                     ACT.Identity, bias=modv[:, sh:sh + 1]).then_inc(hhi_ready, 1)

            act.dma_start(ident[:], t["const_ident"]).then_inc(s_const, 16)
            act.dma_start(xrow[:, 0:XBLK, :], t["x"][0].rearrange("(b p) n -> p b n", p=P)).then_inc(s_x[0], 16)
            act.dma_start(xrow[:, XBLK:NBLK, :], t["ctx"][0].rearrange("(b p) n -> p b n", p=P)).then_inc(s_x[1], 16)
            act.dma_start(mrow[:], t["const_mask"]).then_inc(s_const, 16)
            act.wait_ge(vec_ready, 1)
            for c in range(2):
                ins = nc.scalar.activation(cond[:, c * DC:(c + 1) * DC], vecs[:, 0, ROW_X1 + c * DC:ROW_X1 + (c + 1) * DC],
                                           ACT.Silu)
            ins.then_inc(cond_ready, 1)
            for j in range(DC):
                act.wait_ge(xt_ready, j + 1)
                nc.scalar.activation(x[:, j * NT:(j + 1) * NT], bank(2 * (j % 2), 0, NT), ACT.Copy).then_inc(xt_used, 1)
                act.wait_ge(xt_used, j + 1)
                squares(0, j, BOTH)
            split_hi(0, 0, 0)
            act.wait_ge(set_up, 1)
            norm_apply(0, 0, plan[0], 0, lambda j: htmp[:, j % 2])

            for n_ph, ph in enumerate(plan):
                l, kind, u0, p0 = ph["layer"], ph["kind"], ph["unit"], ph["pair"]
                parts = phase_parts(ph)
                c = sum(pt[1] for pt in parts)
                if kind == "proj":
                    proj_scalar(act, steps, l, u0, p0, split_hi)
                    gla_scalar(act, steps, l, lambda j: hi_chunk(
                        j, 4 * l + 2, l, 1, parts_of("gates", l), lambda k: mf[:, 0, (k % 2) * NT:(k % 2 + 1) * NT]),
                        lambda: split_hi(*second_unit(gates_phase(l))))
                    continue
                for a, b, jobs in segments(ph):
                    def body(i, jobs=jobs):
                        for h in range(2):
                            pair, buf = p0 + 2 * i + h, (p0 + h) % 2
                            unit = u0 + 4 * i + 2 * h
                            for s in range(1, 3):
                                if not (isinstance(i, int) and ph is plan[-1] and 2 * i + h == ph["pairs"] - 1 and s == 2) \
                                        and not is_split_ahead(ph, i, h, s):
                                    split_hi(unit + s, (u0 + 2 * h + s) % 4, (u0 + s) % 2)
                            if kind == "up":
                                act.wait_ge(w_used, unit + 2)
                                for pt in parts:
                                    ins = nc.scalar.activation(stmp[:, h, pt[0]:pt[0] + pt[1]], pair_ps(buf, 0, pt), ACT.Silu)
                                ins.then_inc(silu_done, 1)
                                act.wait_ge(pair_free, pair + 1)
                                nc.scalar.activation(mhi[:, ds((2 * i + h) * NT, c)], mtmp[:, h, 0:c],
                                                     ACT.Copy).then_inc(mhi_done, 1)
                            elif kind == "gates" and h == 0:
                                act.wait_ge(w_used, unit + 2)
                                act.wait_ge(pair_free, pair)
                                if isinstance(i, int) and i == 0:
                                    act.wait_ge(yg_ready, 4 * (l + 1))
                                for s in range(2):
                                    for pt in parts:
                                        ins = nc.scalar.activation(mf[:, s, ds(i * NT + pt[0], pt[1])],
                                                                   pair_ps(buf, s, pt), ACT.Sigmoid)
                                ins.then_inc(pair_free, 1)
                            elif kind == "gates":
                                act.wait_ge(merge_ready, DC * l + i + 1)
                                col = act.snap((i + 1) * NT)
                                nc.scalar.activation(mhi[:, ds(col - NT, c)], mf[:, 1, ds(col - NT, c)],
                                                     ACT.Copy).then_inc(mhi_done, 1)
                            elif last_norm_out(ph):
                                n = norm_of[(l, kind, ph["ffn"])]
                                for s in range(2):
                                    k = SQ_ADDED * n + 4 * i + 2 * h + s
                                    act.wait_ge(pair_free, pair + 1)
                                    act.wait_ge(sq_used, k - 1)
                                    nc.scalar.activation(sq[:, s, 0:c], x[:, ds((4 * i + 2 * h + s) * NT, c)],
                                                         ACT.Square).then_inc(sq_ready, 1)
                    repeat(act, a, b, peeled(ph, a), body)
                if last_norm_out(ph):
                    n = norm_of[(l, kind, ph["ffn"])]
                    if n < 3 * DEPTH:
                        nxt = plan[n_ph + 1]
                        which = {"proj": 1}.get(nxt["kind"], 2 * nxt["ffn"])
                        ap = 4 * nxt["layer"] + (0, 1, 3)[which]
                        norm_apply(ap, n, nxt, which, lambda j: htmp[:, j % 2])
                    else:
                        act.wait_ge(var_ready, n + 1)
                        root(XBLK)
            for j in range(DC):
                act.wait_ge(out_t, j + 1)
                nc.scalar.activation(orow[:, :, j * P:(j + 1) * P], bank(j % 2).rearrange("p (b n) -> p b n", b=XBLK),
                                     ACT.Copy).then_inc(out_row, 1)

        @block.vector
        def _(dve):
            steps = Steps(dve, dve_step)

            def split_lo(unit, slot4, slot2):
                dve.wait_ge(hi_split, unit + 1)
                nc.vector.tensor_tensor(wlo[:, slot2], wraw[:, slot4], whi[:, slot2].bitcast(F32),
                                        ALU.subtract).then_inc(lo_split, 1)

            def mod_accumulate(job, buf, ks):
                if ks[0] == 0:
                    dve.wait_ge(mod_loaded[buf], 8 * job + (16 - 8 * buf - 8 * START_JOBS))
                    at_least(dve, mod_sum, job - 1)
                for k in ks:
                    for c in range(2):
                        if k == 0:
                            ins = nc.vector.tensor_scalar(macc[:, buf, c, :], modraw[:, buf, 0, :],
                                                          cond[:, c * DC:c * DC + 1], None, ALU.mult)
                        else:
                            dve.wait_ge(mod_step, 2 * DC * (job - START_JOBS) + 2 * k - 1 + c)
                            ins = nc.vector.scalar_tensor_tensor(
                                out=macc[:, buf, c, :], in0=modraw[:, buf, k, :],
                                scalar=cond[:, c * DC + k:c * DC + k + 1], in1=macc[:, buf, c, :],
                                op0=ALU.mult, op1=ALU.add)
                        ins.then_inc(mod_step, 1)

            def mod_finish(job, layer):
                dve.wait_ge(mod_sum, job + 1)
                for c in range(2):
                    ins = nc.vector.tensor_tensor(
                        modv[:, ds(c * DEPTH * MODC + 2 * job, 2)], bank(6, 2 * c, 2),
                        vecs[:, layer, ds(ROW_BMOD + 2 * (job - layer * MODJ), 2)], ALU.add)
                ins.then_inc(mod_done, 1)

            def reciprocals(n, nb):
                dve.wait_ge(std_ready, n + 1)
                nc.vector.reciprocal(tok[:, 0:nb], tok[:, 0:nb]).then_inc(rec_ready, 1)
                dve.wait_ge(bc_ready, n + 1)

            def norm_apply(a, nxt, which, tmp, new=True):
                l, parts = nxt["layer"], phase_parts(nxt)
                c = sum(pt[1] for pt in parts)
                if new and a == 0:
                    for i in range(START_JOBS // 2):
                        if i == 2:
                            reciprocals(0, NBLK)
                        dve.wait_ge(mod_sum, 2 * i + 2)
                        nc.vector.tensor_copy(mod_row[0:2, 4 * i * P:4 * (i + 1) * P],
                                              ps[0:2, 512 * FIRST_BANKS[i]:512 * (FIRST_BANKS[i] + 1)]
                                              ).then_inc(first_row, 1)
                    split_lo(0, 0, 0)
                    dve.wait_ge(first_t, START_JOBS // 2)
                    n = 2 * START_JOBS
                    for e in range(2):
                        ins = nc.vector.tensor_tensor(
                            modv[:, e * DEPTH * MODC:e * DEPTH * MODC + n],
                            bank(5, 0, 2 * n).rearrange("p (n c) -> p n c", c=2)[:, :, e],
                            vecs[:, 0, ROW_BMOD:ROW_BMOD + n], ALU.add)
                    ins.then_inc(mod_done, START_JOBS)
                if new:
                    dve.wait_ge(mod_done, mod_needed(l, 3 * which + 2))
                    for e in range(2):
                        sc = e * DEPTH * MODC + l * MODC + (3 * which + 1) * DC
                        steps.link(nc.vector.scalar_tensor_tensor(
                            out=amul[:, e * DC:(e + 1) * DC], in0=modv[:, sc:sc + DC], scalar=1.0,
                            in1=vecs[:, l, ROW_NORM + which * DC:ROW_NORM + (which + 1) * DC],
                            op0=ALU.add, op1=ALU.mult))
                    split_lo(*second_unit(nxt))
                    if a:
                        reciprocals(3 * l + which, c // P)
                    factor = ps[:, 3072:3072 + c]
                else:
                    factor = rstd

                def scaled(i):
                    if i >= 2:
                        dve.wait_ge(h_ready, h_base(a) + i - 1)
                    e, j = divmod(i, DC)
                    t0, m = parts[e]
                    nc.vector.scalar_tensor_tensor(
                        out=tmp(i)[:, t0:t0 + m], in0=x[:, j * NT + t0:j * NT + t0 + m],
                        scalar=amul[:, e * DC + j:e * DC + j + 1], in1=factor[:, t0:t0 + m],
                        op0=ALU.mult, op1=ALU.mult).then_inc(ht_ready, 1)

                def rest(i):
                    dve.wait_ge(hhi_ready, h_base(a) + i + 1)
                    e, j = divmod(i, DC)
                    t0, m = parts[e]
                    sh = e * DEPTH * MODC + l * MODC + 3 * which * DC + j
                    nc.vector.scalar_tensor_tensor(
                        out=hlo[:, j * NT + t0:j * NT + t0 + m], in0=tmp(i)[:, t0:t0 + m],
                        scalar=modv[:, sh:sh + 1], in1=hhi[:, j * NT + t0:j * NT + t0 + m].bitcast(F32),
                        op0=ALU.add, op1=ALU.subtract).then_inc(h_ready, 1)

                chunks = DC * len(parts)

                def step(i):
                    if i < chunks:
                        scaled(i)
                    elif new and which == 1:
                        nc.vector.tensor_copy(rstd[:, 0:c], factor)
                    if i:
                        rest(i - 1)

                work = [lambda i=i: step(i) for i in range(chunks + 1)]
                if not new:
                    return work
                for do in work:
                    do()

            dve.memset(ones[:], 1.0)
            dve.memset(eps[:], EPS).then_inc(set_up, 1)
            dve.wait_ge(vec_t, 1)
            for l in range(DEPTH):
                ins = nc.vector.tensor_copy(vecs[:, l, 0:ROWS[l]], bank(7, l * P, ROWS[l]))
            ins.then_inc(vec_ready, 1)
            dve.wait_ge(cond_ready, 1)
            dve.wait_ge(s_const, 32)
            nc.vector.tensor_copy(masks[:].rearrange("p d n -> p (d n)"), mrow[:])
            norm_apply(0, plan[0], 0, lambda j: htmp[:, j % 2])

            for n_ph, ph in enumerate(plan):
                l, kind, u0, p0, j0 = ph["layer"], ph["kind"], ph["unit"], ph["pair"], ph["job"]
                parts = phase_parts(ph)
                c = sum(pt[1] for pt in parts)
                if kind == "proj":
                    proj_vector(dve, steps, l, u0, p0, split_lo)
                    gla_vector(dve, steps, l, u0, norm_apply(
                        4 * l + 2, plan[n_ph + 1], 1,
                        lambda j: mf[:, 0, (j % 2) * NT:(j % 2 + 1) * NT], new=False),
                        lambda: split_lo(*second_unit(gates_phase(l))))
                    continue
                if (kind == "down" and ph["third"] == 0) or kind == "out":
                    w = {"out": 5}.get(kind, 2 + 6 * ph["ffn"])
                    dve.wait_ge(mod_done, mod_needed(l, w + 1))
                    for e in range(2):
                        g0 = e * DEPTH * MODC + l * MODC + w * DC
                        steps.link(nc.vector.tensor_scalar(gate[:, e * DC:(e + 1) * DC], modv[:, g0:g0 + DC],
                                                           1.0 if kind == "out" else 0.5, None, ALU.mult))
                m0 = m_base(l, ph["ffn"], ph["third"])
                s0 = m0 - DC * (l + ph["ffn"])
                for a, b, jobs in segments(ph):
                    def body(i, jobs=jobs):
                        for h in range(2):
                            pair, buf = p0 + 2 * i + h, (p0 + h) % 2
                            unit, job = u0 + 4 * i + 2 * h, j0 + 2 * i + h
                            if not is_split_ahead(ph, i, h, 1):
                                split_lo(unit + 1, (u0 + 2 * h + 1) % 4, (u0 + 1) % 2)
                            if jobs:
                                mod_accumulate(job, (j0 + h) % 2, range(DC // 2))
                            if not (isinstance(i, int) and ph is plan[-1] and 2 * i + h == ph["pairs"] - 1):
                                split_lo(unit + 2, (u0 + 2 * h + 2) % 4, u0 % 2)
                            if jobs:
                                mod_accumulate(job, (j0 + h) % 2, range(DC // 2, DC))
                            if kind == "up":
                                dve.wait_ge(silu_done, s0 + 2 * i + h + 1)
                                at_least(dve, m_ready, m0 + 2 * i + h - 1)
                                for pt in parts:
                                    ins = nc.vector.tensor_tensor(mtmp[:, h, pt[0]:pt[0] + pt[1]], pair_ps(buf, 1, pt),
                                                                  stmp[:, h, pt[0]:pt[0] + pt[1]], ALU.mult)
                                ins.then_inc(pair_free, 1)
                                dve.wait_ge(mhi_done, m0 + 2 * i + h + 1)
                                nc.vector.tensor_tensor(mlo[:, ds((2 * i + h) * NT, c)], mtmp[:, h, 0:c],
                                                        mhi[:, ds((2 * i + h) * NT, c)].bitcast(F32),
                                                        ALU.subtract).then_inc(m_ready, 1)
                            elif kind in ("down", "out"):
                                dve.wait_ge(w_used, unit + 2)
                                for s in range(2):
                                    n = 4 * i + 2 * h + s
                                    for e, (t0, m) in enumerate(parts):
                                        ins = nc.vector.scalar_tensor_tensor(
                                            out=x[:, ds(n * NT + t0, m)], in0=pair_ps(buf, s, (t0, m)),
                                            scalar=gate[:, ds(e * DC + n, 1)], in1=x[:, ds(n * NT + t0, m)],
                                            op0=ALU.mult, op1=ALU.add)
                                ins.then_inc(pair_free, 1)
                            elif h == 0:
                                pass
                            else:
                                dve.wait_ge(w_used, unit + 2)
                                dve.wait_ge(pair_free, pair)
                                for s in range(2):
                                    for t0, m in parts:
                                        v = mf[:, s, ds(i * NT + t0, m)]
                                        ins = nc.vector.tensor_tensor(v, pair_ps(buf, s, (t0, m)), v, ALU.mult)
                                ins.then_inc(pair_free, 1)
                                dve.wait_ge(pair_free, pair + 1)
                                nc.vector.tensor_tensor(mf[:, 1, ds(i * NT, c)], mf[:, 0, ds(i * NT, c)],
                                                        mf[:, 1, ds(i * NT, c)], ALU.add).then_inc(merge_ready, 1)
                                dve.wait_ge(mhi_done, m_base_merge(l) + i + 1)
                                nc.vector.tensor_tensor(mlo[:, ds(i * NT, c)], mf[:, 1, ds(i * NT, c)],
                                                        mhi[:, ds(i * NT, c)].bitcast(F32),
                                                        ALU.subtract).then_inc(m_ready, 1)
                            if jobs:
                                mod_finish(job, (j0 >= MODJ) * 1)
                    repeat(dve, a, b, peeled(ph, a), body)
                if last_norm_out(ph):
                    n = norm_of[(l, kind, ph["ffn"])]
                    if n < 3 * DEPTH:
                        nxt = plan[n_ph + 1]
                        which = {"proj": 1}.get(nxt["kind"], 2 * nxt["ffn"])
                        norm_apply(4 * nxt["layer"] + (0, 1, 3)[which], nxt, which, lambda j: htmp[:, j % 2])
            reciprocals(3 * DEPTH, XBLK)
            for j in range(DC):
                at_least(dve, out_t, j - 1)
                nc.vector.scalar_tensor_tensor(out=htmp[:, j % 2, 0:SEQ], in0=x[:, j * NT:j * NT + SEQ],
                                               scalar=vecs[:, 1, ROW_X1 + j:ROW_X1 + j + 1], in1=ps[:, 3072:3072 + SEQ],
                                               op0=ALU.mult, op1=ALU.mult).then_inc(ht_ready, 1)

        @block.gpsimd
        def _(pool):
            steps = Steps(pool, pool_step)

            def add_squares(n, j, buf, parts):
                c = sum(pt[1] for pt in parts)
                pool.wait_ge(sq_ready, DC * n + j + 1)
                at_least(pool, sq_used, SQ_ADDED * n + j)
                nc.gpsimd.tensor_tensor(ssq[:, 0:c], ssq[:, 0:c], sq[:, buf, 0:c], ALU.add).then_inc(sq_used, 1)

            def windows(n, w, rows):
                view = lambda i, a, b: padded[i][:, 0:rows * (n + w)].rearrange(
                    "p (r c) -> p r c", c=n + w)[:, :, a:b]
                i, k = 0, 1
                while k < w:
                    m = n + w - 2 * k
                    steps.link(nc.gpsimd.tensor_tensor(view(1 - i, 0, m), view(i, 0, m), view(i, k, k + m), ALU.add))
                    i, k = 1 - i, 2 * k
                return view(i, 0, n), view(1 - i, 0, n)

            def pad_edges(n, w, rows):
                v = padded[0][:, 0:rows * (n + w)].rearrange("p (r c) -> p r c", c=n + w)
                steps.link(nc.gpsimd.memset(v[:, :, 0:w // 2], 0.0))
                steps.link(nc.gpsimd.memset(v[:, :, n + w // 2:n + w], 0.0))
                return v[:, :, w // 2:n + w // 2]

            def pool_groups(l, p0):
                pool.wait_ge(s_mix, 16 * 5 * (l + 1))
                for g, w in enumerate(WINDOWS):
                    pool.wait_ge(pair_free, p0 + 4 + g // 2)
                    src = u[:, g, :]
                    if w // 2 >= GRID_H:
                        rows, n = 1, SEQ // 2
                        steps.link(nc.gpsimd.tensor_tensor(racc[:, 0:n], src[:, 0:n], src[:, n:2 * n], ALU.add))
                        while n > GRID_W:
                            n //= 2
                            steps.link(nc.gpsimd.tensor_tensor(racc[:, 0:n], racc[:, 0:n], racc[:, n:2 * n], ALU.add))
                    else:
                        rows = GRID_H
                        steps.link(nc.gpsimd.tensor_copy(racc[:, 0:GRID_W], src[:, 0:GRID_W]))
                        steps.link(nc.gpsimd.tensor_tensor(racc[:, GRID_W:], src[:, GRID_W:SEQ],
                                                           src[:, 0:SEQ - GRID_W], ALU.add))
                        for o in range(-(w // 2), w // 2):
                            if o not in (-1, 0):
                                a, b = max(0, -o) * GRID_W, (GRID_H - max(0, o)) * GRID_W
                                steps.link(nc.gpsimd.tensor_tensor(racc[:, a:b], racc[:, a:b],
                                                                   src[:, a + o * GRID_W:b + o * GRID_W], ALU.add))
                    inner = pad_edges(GRID_W, w, rows)
                    steps.link(nc.gpsimd.tensor_tensor(
                        inner, racc[:, 0:rows * GRID_W].rearrange("p (r c) -> p r c", c=GRID_W),
                        recs[:, g, 0:rows, None].to_broadcast([P, rows, GRID_W]), ALU.mult))
                    sums, free = windows(GRID_W, w, rows)
                    steps.link(nc.gpsimd.tensor_tensor(
                        free, sums, recs[:, g, None, GRID_H:].to_broadcast([P, rows, GRID_W]), ALU.mult))
                    tokens = src[:, 0:SEQ].rearrange("p (r c) -> p r c", c=GRID_W)
                    if rows == 1:
                        free = free.to_broadcast([P, GRID_H, GRID_W])
                    ins = nc.gpsimd.tensor_tensor(tokens, free, tokens, ALU.subtract)
                    if l < DEPTH - 1:
                        steps.link(ins)
                        inner = pad_edges(CTX, w, 1)
                        steps.link(nc.gpsimd.tensor_copy(inner, src[:, None, SEQ:NT]))
                        sums, free = windows(CTX, w, 1)
                        half = GRID_W // 2
                        for a, b, rec in ((0, half, recs[:, g, None, GRID_H:GRID_H + half]),
                                          (CTX - half, CTX, recs[:, g, None, GRID_H + half:]),
                                          (half, CTX - half, recs[:, g, None, GRID_H + half - 1:GRID_H + half]
                                           .to_broadcast([P, 1, CTX - 2 * half]))):
                            steps.link(nc.gpsimd.tensor_tensor(free[:, :, a:b], sums[:, :, a:b], rec, ALU.mult))
                        ins = nc.gpsimd.tensor_tensor(src[:, None, SEQ:NT], free, src[:, None, SEQ:NT], ALU.subtract)
                    ins.then_inc(pooled, 1)
                    pool.wait_ge(pooled, 4 * l + g + 1)

            def clear_squares(n):
                if n:
                    pool.wait_ge(var_ready, n)
                steps.link(nc.gpsimd.memset(ssq[:], 0.0))

            clear_squares(0)
            for j in range(SQ_ADDED):
                add_squares(0, j, j % 2, BOTH)
            for ph in plan:
                l, kind, u0, p0 = ph["layer"], ph["kind"], ph["unit"], ph["pair"]
                if kind == "proj":
                    pool_groups(l, p0)
                    pool.wait_ge(misc_ready, MISC * (l + 1))
                    steps.link(nc.gpsimd.memset(att[:], 0.0))
                    pool.wait_ge(w_used, u0 + ph["units"])
                    steps.link(nc.gpsimd.memset(kpad[CHUNK:P, :, :, 0, :], 0.0))
                    nc.gpsimd.memset(kpad[0:CHUNK, :, :, 1, :], 0.0).then_inc(gla_zero, 1)
                    pool.wait_ge(gla_zero, 2 * l + 1)
                    steps.link(nc.gpsimd.memset(qbd[DK:P, :, 0, :], 0.0))
                    nc.gpsimd.memset(qbd[0:DK, :, 1, :], 0.0).then_inc(gla_zero, 1)
                    pool.wait_ge(gla_zero, 2 * l + 2)
                    c = blocks(l) * P
                    for h in range(HEADS):
                        pool.wait_ge(o_used, o_before(l, h // 2) + blocks(l))
                        nc.gpsimd.tensor_tensor(rsil[:, h, 0:c], bsum[:, h, 0:c], rsil[:, h, 0:c],
                                                ALU.mult).then_inc(oscaled, 1)
                        pool.wait_ge(oscaled, 4 * l + h + 1)
                elif last_norm_out(ph):
                    n = norm_of[(l, kind, ph["ffn"])]
                    pool.wait_ge(w_used, u0 + 2)
                    clear_squares(n)

                    for j in range(SQ_ADDED):
                        add_squares(n, j, j % 2, phase_parts(ph))



_INS = ["x", "c", "ctx", "c_ctx", "w_mod", "b_mod", "norm_w", "ffn1_up", "ffn1_down", "w_in", "w_af_up", "b_af",
        "w_ab_up", "b_ab", "gla_norm_w", "pool_w", "pool_scale", "w_br_pool", "w_br_gla", "w_out",
        "ffn2_up", "ffn2_down", "final_norm_w"]


def constants():
    source, target = np.arange(P)[:, None], np.arange(P)[None, :]
    same = source // CHUNK == target // CHUNK
    forward, backward = same & (source <= target), same & (source > target)
    mask = np.concatenate([forward, forward, backward, backward], axis=1).astype(np.float32)
    recs = []
    for w in WINDOWS:
        sizes = [np.clip(np.arange(n) + w // 2, 0, n) - np.clip(np.arange(n) - w // 2, 0, n) for n in (GRID_H, GRID_W)]
        recs.append(1.0 / np.concatenate(sizes))
    return {
        "const_ident": np.eye(P, dtype=np.float32),
        "const_mask": mask,
        "const_reset": (np.arange(NT) % CHUNK != 0).astype(np.float32),
        "const_pool": np.array(recs, np.float32),
    }


def kernel(**inputs):
    import concourse.bacc as _bacc
    from concourse.bass_utils import run_bass_kernel_spmd as _run

    nc = _bacc.Bacc("TRN2", target_bir_lowering=False, num_devices=1)
    arrays, t = {}, {}
    named = {n: np.ascontiguousarray(inputs[n]) for n in _INS}
    named.update(constants())
    for name, a in named.items():
        arrays[f"in_{name}"] = a
        t[name] = nc.dram_tensor(f"in_{name}", a.shape, mybir.dt.from_np(a.dtype), kind="ExternalInput").ap()
    t["out"] = nc.dram_tensor("out_dram", (1, SEQ, D), F32, kind="ExternalOutput").ap()
    build(nc, t)
    r = _run(nc, [arrays], core_ids=[0])
    return r.results[0]["out_dram"]
```
